# Optimizing a Trainium2 kernel written in Bass

```python
import jax, jax.numpy as jnp
from jax import lax
import numpy as np

D_MODEL = 1024
BATCH = 1
SEQ = 512
DEPTH = 2
DEC_BATCH = 1
DEC_SEQ = 32
PAST_LEN = 256

CHUNK = 64
D_MIX = D_MODEL
D_POOL = D_MIX // 4
POOL_WINDOWS = (2, 4, 8, 16)
POOL_GROUP = D_POOL // len(POOL_WINDOWS)
POOL_HIST = max(POOL_WINDOWS) - 1
D_CONF = (D_MIX - D_POOL) // 2
CONF_WIDTH = 31
D_SC = D_MIX - D_POOL - D_CONF
SC_WIDTH = 3
D_IN = D_POOL + 2 * D_CONF + 3 * D_SC
PEER_HEADS = 8
PEER_NKEYS = 128
PEER_EXPERTS = PEER_NKEYS * PEER_NKEYS
PEER_TOPK = 16
PEER_DKEY = 128
PEER_DHALF = PEER_DKEY // 2
PEER_BLOCK = 128
EPS = 1e-6

kernel_name = 'hybrid_pool_conformer_shortconv_peer_step'

def rms_norm(x, g):
    xf = x.astype(jnp.float32)
    y = xf * lax.rsqrt(jnp.mean(xf * xf, axis=-1, keepdims=True) + EPS)
    return (y * g.astype(jnp.float32)).astype(x.dtype)

def layer_norm(x, g, b):
    xf = x.astype(jnp.float32)
    mu = jnp.mean(xf, axis=-1, keepdims=True)
    var = jnp.mean(jnp.square(xf - mu), axis=-1, keepdims=True)
    y = (xf - mu) * lax.rsqrt(var + EPS)
    return (y * g.astype(jnp.float32) + b.astype(jnp.float32)).astype(x.dtype)

def causal_depthwise(z, hist, w):
    width = w.shape[0]
    zp = jnp.concatenate([hist.astype(z.dtype), z], axis=1)
    y = lax.conv_general_dilated(zp, w[:, None, :].astype(z.dtype), window_strides=(1,), padding='VALID',
                                 dimension_numbers=('NWC', 'WIO', 'NWC'), feature_group_count=z.shape[-1])
    return y, zp[:, zp.shape[1] - (width - 1):]

def pool_mixer(u, hist, start, w_pool, scale):
    bsz, L, _ = u.shape
    up = jnp.concatenate([hist.astype(u.dtype), u], axis=1)
    csp = jnp.pad(jnp.cumsum(up.astype(jnp.float32), axis=1), ((0, 0), (1, 0), (0, 0)))
    pos = jnp.arange(L, dtype=jnp.float32) + start
    off = POOL_HIST + 1
    parts = []
    for g, w in enumerate(POOL_WINDOWS):
        sl = slice(g * POOL_GROUP, (g + 1) * POOL_GROUP)
        s = csp[:, off:off + L, sl] - csp[:, off - w:off - w + L, sl]
        cnt = jnp.minimum(pos + 1.0, float(w))
        parts.append(s / cnt[None, :, None])
    mean = jnp.concatenate(parts, axis=-1)
    d = (mean - u.astype(jnp.float32)).astype(u.dtype).reshape(bsz, L, len(POOL_WINDOWS), POOL_GROUP)
    y = jnp.einsum('blgc,gcd->blgd', d, w_pool).reshape(bsz, L, D_POOL) * scale
    return y, up[:, up.shape[1] - POOL_HIST:]

def mixer(h, hist_pool, hist_dw, hist_sc, start, w_in, w_pool, pool_scale, w_dw, b_dw, ln_g, ln_b, w_sc, w_out):
    p = h @ w_in
    cuts = [D_POOL, D_POOL + D_CONF, D_POOL + 2 * D_CONF, D_POOL + 2 * D_CONF + D_SC, D_POOL + 2 * D_CONF + 2 * D_SC]
    u_pool, c_val, c_gate, s_h, s_b, s_c = jnp.split(p, cuts, axis=-1)
    y_a, nh_pool = pool_mixer(u_pool, hist_pool, start, w_pool, pool_scale)
    z = c_val * jax.nn.sigmoid(c_gate)
    zc, nh_dw = causal_depthwise(z, hist_dw, w_dw)
    y_b = jax.nn.silu(layer_norm(zc + b_dw, ln_g, ln_b))
    ys, nh_sc = causal_depthwise(s_c * s_h, hist_sc, w_sc)
    y_c = s_b * ys
    out = jnp.concatenate([y_a, y_b, y_c], axis=-1) @ w_out
    return out, nh_pool, nh_dw, nh_sc

def peer(h, w_q, sub_keys, expert_u, expert_v):
    bsz, L, D = h.shape
    T = bsz * L
    t = h.reshape(T, D)
    q = (t @ w_q).reshape(T, PEER_HEADS, 2, PEER_DHALF)
    s = jnp.einsum('thpd,hpnd->thpn', q, sub_keys)
    ts, ti = lax.top_k(s, PEER_TOPK)
    cand_s = (ts[:, :, 0, :, None] + ts[:, :, 1, None, :]).reshape(T, PEER_HEADS, PEER_TOPK * PEER_TOPK)
    cand_i = (ti[:, :, 0, :, None] * PEER_NKEYS + ti[:, :, 1, None, :]).reshape(T, PEER_HEADS, PEER_TOPK * PEER_TOPK)
    best_s, best_j = lax.top_k(cand_s, PEER_TOPK)
    ids = jnp.take_along_axis(cand_i, best_j, axis=-1)
    gates = jax.nn.softmax(best_s.astype(jnp.float32), axis=-1).astype(h.dtype)
    blk = min(PEER_BLOCK, T)
    nblk = -(-T // blk)
    pad = nblk * blk - T
    tb = jnp.pad(t, ((0, pad), (0, 0))).reshape(nblk, blk, D)
    ib = jnp.pad(ids, ((0, pad), (0, 0), (0, 0))).reshape(nblk, blk, PEER_HEADS, PEER_TOPK)
    gb = jnp.pad(gates, ((0, pad), (0, 0), (0, 0))).reshape(nblk, blk, PEER_HEADS, PEER_TOPK)

    def expert_block(args):
        xb, idb, gtb = args
        act = jax.nn.gelu(jnp.einsum('td,thkd->thk', xb, expert_u[idb]), approximate=False)
        return jnp.einsum('thk,thkd->td', gtb * act, expert_v[idb])

    out = lax.map(expert_block, (tb, ib, gb)).reshape(nblk * blk, D)[:T]
    return out.reshape(bsz, L, D)

def setup_inputs(seed: int = 0) -> dict:
    key = jax.random.key(seed)
    ks = jax.random.split(key, 24)

    def nrm(k, shape, scale):
        return jax.random.normal(k, shape, jnp.float32) * scale

    return {
        'x_prompt': nrm(ks[0], (BATCH, SEQ, D_MODEL), 1.0),
        'x_sample': nrm(ks[1], (DEC_BATCH, DEC_SEQ, D_MODEL), 1.0),
        'state_pool': nrm(ks[2], (DEPTH, DEC_BATCH, POOL_HIST, D_POOL), 1.0),
        'state_dwconv': nrm(ks[3], (DEPTH, DEC_BATCH, CONF_WIDTH - 1, D_CONF), 0.5),
        'state_shortconv': nrm(ks[4], (DEPTH, DEC_BATCH, SC_WIDTH - 1, D_SC), 1.0),
        'g_mix': 1.0 + nrm(ks[5], (DEPTH, D_MODEL), 0.02),
        'w_in': nrm(ks[6], (DEPTH, D_MODEL, D_IN), D_MODEL ** -0.5),
        'w_pool': nrm(ks[7], (DEPTH, len(POOL_WINDOWS), POOL_GROUP, POOL_GROUP), POOL_GROUP ** -0.5),
        'pool_scale': 1.0 + nrm(ks[8], (DEPTH, D_POOL), 0.02),
        'w_dw': nrm(ks[9], (DEPTH, CONF_WIDTH, D_CONF), CONF_WIDTH ** -0.5),
        'b_dw': nrm(ks[10], (DEPTH, D_CONF), 0.02),
        'ln_g': 1.0 + nrm(ks[11], (DEPTH, D_CONF), 0.02),
        'ln_b': nrm(ks[12], (DEPTH, D_CONF), 0.02),
        'w_sc': nrm(ks[13], (DEPTH, SC_WIDTH, D_SC), SC_WIDTH ** -0.5),
        'w_out': nrm(ks[14], (DEPTH, D_MIX, D_MODEL), D_MIX ** -0.5),
        'g_ffn': 1.0 + nrm(ks[15], (DEPTH, D_MODEL), 0.02),
        'w_q': nrm(ks[16], (DEPTH, D_MODEL, PEER_HEADS * PEER_DKEY), D_MODEL ** -0.5),
        'sub_keys': nrm(ks[17], (DEPTH, PEER_HEADS, 2, PEER_NKEYS, PEER_DHALF), PEER_DHALF ** -0.5),
        'expert_u': nrm(ks[18], (DEPTH, PEER_EXPERTS, D_MODEL), D_MODEL ** -0.5),
        'expert_v': nrm(ks[19], (DEPTH, PEER_EXPERTS, D_MODEL), PEER_HEADS ** -0.5),
        'g_final': 1.0 + nrm(ks[20], (D_MODEL,), 0.02),
    }

def reference(x_prompt, x_sample, state_pool, state_dwconv, state_shortconv, g_mix, w_in, w_pool, pool_scale,
              w_dw, b_dw, ln_g, ln_b, w_sc, w_out, g_ffn, w_q, sub_keys, expert_u, expert_v, g_final):
    xp, xs = x_prompt, x_sample
    bp = x_prompt.shape[0]
    zp_pool = jnp.zeros((bp, POOL_HIST, D_POOL), x_prompt.dtype)
    zp_dw = jnp.zeros((bp, CONF_WIDTH - 1, D_CONF), x_prompt.dtype)
    zp_sc = jnp.zeros((bp, SC_WIDTH - 1, D_SC), x_prompt.dtype)
    pool_p, dw_p, sc_p, pool_s, dw_s, sc_s = [], [], [], [], [], []
    for l in range(DEPTH):
        m, a, b, c = mixer(rms_norm(xp, g_mix[l]), zp_pool, zp_dw, zp_sc, 0, w_in[l], w_pool[l], pool_scale[l],
                           w_dw[l], b_dw[l], ln_g[l], ln_b[l], w_sc[l], w_out[l])
        xp = xp + m
        xp = xp + peer(rms_norm(xp, g_ffn[l]), w_q[l], sub_keys[l], expert_u[l], expert_v[l])
        pool_p.append(a); dw_p.append(b); sc_p.append(c)
        m, a, b, c = mixer(rms_norm(xs, g_mix[l]), state_pool[l], state_dwconv[l], state_shortconv[l], PAST_LEN,
                           w_in[l], w_pool[l], pool_scale[l], w_dw[l], b_dw[l], ln_g[l], ln_b[l], w_sc[l], w_out[l])
        xs = xs + m
        xs = xs + peer(rms_norm(xs, g_ffn[l]), w_q[l], sub_keys[l], expert_u[l], expert_v[l])
        pool_s.append(a); dw_s.append(b); sc_s.append(c)
    y_prompt = rms_norm(xp, g_final)
    y_sample = rms_norm(xs, g_final)
    return (y_prompt, y_sample, jnp.stack(pool_p), jnp.stack(dw_p), jnp.stack(sc_p),
            jnp.stack(pool_s), jnp.stack(dw_s), jnp.stack(sc_s))


_drawn_inputs = setup_inputs


def setup_inputs(seed=0):
    import zlib

    import numpy as np

    out = dict(_drawn_inputs(seed))
    spreads = {}
    factors = {'ln_b': 2.804, 'g_final': 2.953}
    for name, (base, spread) in spreads.items():
        noise = np.random.default_rng([zlib.crc32(name.encode()), seed]).standard_normal(out[name].shape)
        drawn = base * np.exp(spread * noise) if base else spread * noise
        out[name] = __import__('jax').numpy.asarray(drawn.astype(out[name].dtype))
    for name, factor in factors.items():
        out[name] = (out[name] * factor).astype(out[name].dtype)
    return out
```

```python
from contextlib import ExitStack

import concourse.bass as bass
from concourse import mybir

ALU = mybir.AluOpType
ACT = mybir.ActivationFunctionType
AX = mybir.AxisListType
F32 = mybir.dt.float32
BF16 = mybir.dt.bfloat16
U32 = mybir.dt.uint32
I32 = mybir.dt.int32

P = 128
RING = 4
PARTS = 16
EPS = 1e-6
LOWEST = -3.0e38


def ds4(t, base):
    return bass.ds(t * RING + base, RING)


def build(nc, A, O):
    DEPTH, D = A["g_mix"].shape
    SEQ, LS = A["x_prompt"].shape[1], A["x_sample"].shape[1]
    DP, DC, DSC = A["state_pool"].shape[3], A["state_dwconv"].shape[3], A["state_shortconv"].shape[3]
    HP, HC, HS = A["state_pool"].shape[2], A["state_dwconv"].shape[2], A["state_shortconv"].shape[2]
    NE = A["expert_u"].shape[1]
    HEADS, NK, DH = A["sub_keys"].shape[1], A["sub_keys"].shape[3], A["sub_keys"].shape[4]
    TOPK = 16
    KPICK = HEADS * TOPK
    DC8 = D // P
    CP, CC, CS = DP // P, DC // P, DSC // P
    D_IN = DP + 2 * DC + 3 * DSC
    WINDOWS = (2, 4, 8, 16)
    TILES = SEQ // P + 1
    ITEMS = DEPTH * TILES
    COPIES = P // LS
    assert (CP, CC, CS, DC8, KPICK, NK, DH, COPIES) == (2, 3, 3, 8, 128, 128, 64, 4)

    def is_sample(m):
        return m % TILES == TILES - 1

    def width(m):
        return LS if is_sample(m) else P

    def loads(m):
        return COPIES if is_sample(m) else 1

    def groups(m):
        return (KPICK // COPIES if is_sample(m) else KPICK) // RING

    def group_span(m, part):
        g = groups(m)
        return part * g // PARTS + (part * g % PARTS > 0), \
            ((part + 1) * g + PARTS - 1) // PARTS - (part * g + PARTS - 1) // PARTS

    def before(m):
        return sum(groups(i) for i in range(m))

    def outputs_state(m):
        return m % TILES >= TILES - 2

    def state_count(m):
        return sum(outputs_state(i) for i in range(m + 1))

    eu = A["expert_u"].rearrange("l e d -> (l e) d")
    ev = A["expert_v"].rearrange("l e d -> (l e) d")

    with ExitStack() as ctx:
        def sb(name, shape, dt=F32):
            return ctx.enter_context(nc.sbuf_tensor(name, shape, dt))

        def ps(name):
            return ctx.enter_context(nc.psum_tensor(name, [P, 1024], F32))

        def sem(name):
            return ctx.enter_context(nc.semaphore(name))

        w_in = sb("w_in_sb", [P, DC8, D_IN])
        w_out = sb("w_out_sb", [P, DC8, D])
        w_q = sb("w_q_sb", [P, DC8, D])
        keysT = sb("keysT", [P, HEADS, NK])
        urows = sb("urows", [P, RING, D])
        vrows = sb("vrows", [P, RING, D])
        diag = sb("diag", [P, RING, P])
        h_cur = sb("h_cur", [P, D])
        x_mix = sb("x_mix", [P, D])
        x_out = sb("x_out", [P, D])
        g_fin = sb("g_fin", [P, D])
        hT = sb("hT", [P, DC8, P])
        yT = sb("yT", [P, DC8, P])
        qT = yT
        work = sb("work", [P, 2048])
        zbuf = sb("zbuf", [P, CC, HC + P])
        ubuf = sb("ubuf", [P, CP, HP + P])
        mbuf = sb("mbuf", [P, CS, HS + P])
        ids = sb("ids", [P, 3, KPICK], U32)
        gates = sb("gates", [P, 2, KPICK])
        dots = sb("dots", [P, KPICK])
        dots4 = sb("dots4", [P, RING])
        gelu = sb("gelu", [P, KPICK])
        coef = sb("coef", [P, KPICK])
        coef4 = sb("coef4", [P, RING])
        idf = sb("idf", [P, KPICK])
        best = sb("best", [P, KPICK])
        ident = sb("ident", [P, P])
        fold = sb("fold", [P, P])
        ones = sb("ones", [P, P])
        zeros = sb("zeros", [P, 512], BF16)
        w_pool = sb("w_pool_sb", [P, DEPTH, CP, P])
        chan = sb("chan", [P, DEPTH, CC, HC + 1 + 3 + HS + 1])
        gain = sb("gain", [P, DEPTH, 2 * DC8 + CP])
        stat = sb("stat", [P, 8])
        hsum = sb("hsum", [P, HEADS])
        iota_i = sb("iota_i", [P, TOPK], I32)
        iota_f = sb("iota_f", [P, TOPK])
        rcnt = sb("rcnt", [P, CP, TOPK])
        idx_u = sb("idx_u", [P, RING], U32)
        idx_v = sb("idx_v", [P, RING], U32)
        eps = sb("eps", [P, 1])
        x_mid = nc.dram_tensor("x_mid", [SEQ + LS, D], F32).ap()

        NCH = HC + 1 + 3 + HS + 1
        TAP, BIAS, LNG, LNB, STAP = 0, HC + 1, HC + 2, HC + 3, HC + 4

        xn = work[:, 0:1024]
        upper = work[:, 1024:2048]
        zc = work[:, 0:384].rearrange("p (c t) -> p c t", c=CC)
        sig = work[:, 384:768].rearrange("p (c t) -> p c t", c=CC)
        lnstd = work[:, 384:512]
        win_a = work[:, 768:768 + CP * (HP + P)].rearrange("p (c t) -> p c t", c=CP)
        win_b = work[:, 1056:1056 + CP * (HP + P)].rearrange("p (c t) -> p c t", c=CP)
        pdif = work[:, 1344:1600].rearrange("p (c t) -> p c t", c=CP)
        shc = work[:, 1600:1984].rearrange("p (c t) -> p c t", c=CS)
        cand = work[:, 0:512].rearrange("p (h a b) -> p h a b", h=2, a=TOPK)
        wk256 = work[:, 512:768]
        onehot = work[:, 768:1280].rearrange("p (h s m) -> p h s m", h=2, s=TOPK)
        wk128 = work[:, 1280:1408]
        tv = work[:, 1408:1472].rearrange("p (h q k) -> p h q k", h=2, q=2)
        ti = work[:, 1472:1536].bitcast(U32).rearrange("p (h q k) -> p h q k", h=2, q=2)
        tif = work[:, 1536:1600].rearrange("p (h q k) -> p h q k", h=2, q=2)
        bj = work[:, 1600:1632].bitcast(U32).rearrange("p (h k) -> p h k", h=2)
        ab = work[:, 1632:1696].bitcast(U32).rearrange("p (q h k) -> p q h k", q=2, h=2)
        abf = work[:, 1696:1760].rearrange("p (q h k) -> p q h k", q=2, h=2)
        ij = work[:, 1760:1824].rearrange("p (q h k) -> p q h k", q=2, h=2)

        psA, psB, psC, yacc = ps("psA"), ps("psB"), ps("psC"), ps("yacc")

        def tri(ap):
            return ap.rearrange("p (c t) -> p c t", t=P)

        p_gate, p_val = tri(psB[:, 0:384]), tri(psB[:, 512:896])
        p_u, p_sh = tri(psC[:, 0:256]), tri(psC[:, 512:896])
        p_sc, p_sb = tri(psA[:, 0:384]), tri(psA[:, 512:896])
        PROJ = []
        for dst, first, n in ((p_gate, DP + DC, CC), (p_val, DP, CC), (p_u, 0, CP),
                              (p_sh, DP + 2 * DC, CS), (p_sc, DP + 2 * DC + 2 * DSC, CS),
                              (p_sb, DP + 2 * DC + DSC, CS)):
            PROJ += [(first + c * P, dst, c) for c in range(n)]
        PROJ_PARTS = {2: PROJ[0:4], 3: PROJ[4:8], 4: PROJ[8:12], 5: PROJ[12:17]}
        STATE_CHUNKS = [(ubuf, c, HP) for c in range(CP)] + [(zbuf, c, HC) for c in range(CC)] + \
                       [(mbuf, c, HS) for c in range(CS)]

        s_const = sem("consts_made")
        s_fold = sem("fold_made")
        s_zero = sem("zeros_made")
        s_prm = sem("params_loaded")
        s_prmT = sem("params_turned")
        s_prmS = sem("params_stored")
        s_gfin = sem("g_final_loaded")
        s_wpz = sem("w_pool_cleared")
        s_wp = sem("w_pool_loaded")
        s_wi = [sem("w_in_loaded_a"), sem("w_in_loaded_b")]
        s_wo = sem("w_out_loaded")
        s_wq = sem("w_q_loaded")
        s_kst = sem("keys_loaded")
        s_ktT = sem("keys_turned")
        s_kT = sem("keys_stored")
        s_hst = sem("states_loaded")
        s_hstT = sem("states_turned")
        s_hist = sem("histories_set")
        s_x = sem("x_loaded")
        s_std1 = sem("x_std")
        s_xn = sem("x_normed")
        s_t1 = sem("x_turned")
        s_hT = sem("hT_set")
        s_proj = sem("projected")
        s_sig = sem("gate_sigmoid")
        s_zc = sem("conv_done")
        s_mean = sem("ln_sum")
        s_d = sem("ln_centred")
        s_sq = sem("ln_squared")
        s_var = sem("ln_sum_sq")
        s_lstd = sem("ln_std")
        s_xhat = sem("ln_normed")
        s_pd = sem("pool_diff")
        s_ya = sem("pool_mixed")
        s_sh = sem("s_h_copied")
        s_yab = sem("yT_pool_conf_set")
        s_yc = sem("yT_short_set")
        s_nst = sem("new_states_turned")
        s_nsc = sem("new_states_copied")
        s_nso = sem("new_states_stored")
        s_wod = sem("w_out_done")
        s_x1 = sem("x_mixed")
        s_xst = sem("x_mixed_stored")
        s_std2 = sem("x1_std")
        s_xn2 = sem("x1_normed")
        s_t2 = sem("x1_turned")
        s_hT2 = sem("ffn_hT_set")
        s_bt = sem("h_turned_back")
        s_h = sem("h_set")
        s_q = sem("queries_made")
        s_qT = sem("queries_copied")
        s_sc = sem("scores_made")
        s_e = sem("gate_logits")
        s_exp = sem("gate_exp")
        s_ids = sem("ids_ready")
        s_hcur = sem("h_cur_set")
        s_dots = sem("dots_copied")
        s_gelu = sem("gelu_done")
        s_coef = sem("coef_ready")
        s_urow = [sem(f"u_row_landed_{j}") for j in range(RING)]
        s_vrow = [sem(f"v_row_landed_{j}") for j in range(RING)]
        s_ufree = sem("u_rows_free")
        s_vfree = sem("v_rows_free")
        s_ustg = sem("u_indices_staged")
        s_vstg = sem("v_indices_staged")
        s_go = sem("pool_goes_on")
        s_coef4 = sem("coef4_staged")
        s_diag = sem("diag_made")
        s_ysum = sem("v_rows_summed")
        s_xo = sem("x_out_loaded")
        s_yend = sem("x_out_added")
        s_fstd = sem("final_std")
        s_fin = sem("final_normed")
        s_xost = sem("x_out_stored")
        dve_step = sem("dve_step")
        act_step = sem("act_step")

        block = ctx.enter_context(nc.Block())

        def rows_of(m):
            k = m % TILES
            return slice(k * P, k * P + width(m))

        def x_source(m):
            if m >= TILES:
                return x_mid[rows_of(m), :]
            if is_sample(m):
                return A["x_sample"][0, :, :]
            return A["x_prompt"][0, m * P:(m + 1) * P, :]

        def run_part(eng, n, part, body, uses="uv"):
            u = v = None
            nu = nv = 0
            if n < ITEMS and "u" in uses:
                g, nu = group_span(n, part)
                u = (n, g, before(n) + g)
            if n >= 1 and "v" in uses:
                g, nv = group_span(n - 1, part)
                v = (n - 1, g, before(n - 1) + g)
            runs = [(nu, u, v)] if nu == nv else [(nu, u, None), (nv, None, v)]
            for count, a, b in runs:
                if count > 1:
                    with eng.Fori(0, count) as t:
                        body(t, a, b)
                elif count:
                    body(0, a, b)

        @block.sync
        def _(sp):
            def load_w_in(l, half):
                cols = slice(0, DP + 2 * DC) if half == 0 else slice(DP + 2 * DC, D_IN)
                sp.dma_start(w_in[:, :, cols], A["w_in"][l].rearrange("(c p) n -> p c n", p=P)[:, :, cols])\
                    .then_inc(s_wi[half], 16)

            def load_w(dst, name, l, s):
                sp.dma_start(dst[:, :, :], A[name][l].rearrange("(c p) n -> p c n", p=P)).then_inc(s, 16)

            def load_keys(l):
                sp.dma_start(upper.rearrange("p (h q d) -> p h q d", h=HEADS, q=2),
                             A["sub_keys"][l].rearrange("h q n d -> n h q d")).then_inc(s_kst, 16)

            def load_x(m):
                if m >= TILES:
                    sp.wait_ge(s_xost, 16 * (m - TILES + 1))
                for q in range(loads(m)):
                    rows = width(m)
                    sp.dma_start(x_mix[q * rows:(q + 1) * rows, :], x_source(m)).then_inc(s_x, 16)

            def superstep_start(n):
                m = n + 1
                if m < ITEMS:
                    sp.wait_ge(s_hcur, n + 1)
                    load_x(m)
                    sp.wait_ge(s_ids, m)
                    if m % TILES == 0:
                        load_keys(m // TILES)
                    if is_sample(m):
                        l = m // TILES
                        sp.dma_start(upper[0:HP, 0:DP], A["state_pool"][l, 0]).then_inc(s_hst, 16)
                        sp.dma_start(upper[0:HC, DP:DP + DC], A["state_dwconv"][l, 0]).then_inc(s_hst, 16)
                        sp.dma_start(upper[0:HS, DP + DC:D], A["state_shortconv"][l, 0]).then_inc(s_hst, 16)
                if n >= 2:
                    store_out(n - 2)
                if n >= 1:
                    if n >= 2:
                        sp.wait_ge(s_xost, 16 * (n - 1))
                    sp.wait_ge(s_xst, 16 * n)
                    sp.dma_start(x_out[0:width(n - 1), :], x_mid[rows_of(n - 1), :]).then_inc(s_xo, 16)

            def store_out(v):
                if v < TILES:
                    sp.wait_ge(s_yend, v + 1)
                    dst = x_mid[rows_of(v), :]
                else:
                    sp.wait_ge(s_fin, v - TILES + 1)
                    k = v % TILES
                    dst = O["y_sample"][0] if is_sample(v) else O["y_prompt"][0, k * P:(k + 1) * P, :]
                sp.dma_start(dst, x_out[0:width(v), :]).then_inc(s_xost, 16)

            def mixer_io(m):
                l = m // TILES
                if outputs_state(m):
                    o = "sample" if is_sample(m) else "prompt"
                    sp.wait_ge(s_nsc, state_count(m))
                    sp.dma_start(O["new_pool_" + o][l, 0], upper[0:HP, 0:DP]).then_inc(s_nso, 16)
                    sp.dma_start(O["new_dwconv_" + o][l, 0], upper[0:HC, DP:DP + DC]).then_inc(s_nso, 16)
                    sp.dma_start(O["new_shortconv_" + o][l, 0], upper[0:HS, DP + DC:D]).then_inc(s_nso, 16)
                more = is_sample(m) and l + 1 < DEPTH
                if more:
                    sp.wait_ge(s_proj, 4 * (m + 1))
                    load_w_in(l + 1, 0)
                    load_w_in(l + 1, 1)
                sp.wait_ge(s_x1, m + 1)
                sp.dma_start(x_mid[rows_of(m), :], x_mix[0:width(m), :]).then_inc(s_xst, 16)
                if more:
                    sp.wait_ge(s_wod, m + 1)
                    load_w(w_out, "w_out", l + 1, s_wo)
                    sp.wait_ge(s_q, 2 * (m + 1))
                    load_w(w_q, "w_q", l + 1, s_wq)

            load_x(0)
            for l in range(DEPTH):
                taps = urows[0:NCH, 0, l * DC:(l + 1) * DC]
                sp.dma_start(taps[TAP:TAP + HC + 1, :], A["w_dw"][l]).then_inc(s_prm, 16)
                sp.dma_start(taps[BIAS:BIAS + 1, :], A["b_dw"][l:l + 1, :]).then_inc(s_prm, 16)
                sp.dma_start(taps[LNG:LNG + 1, :], A["ln_g"][l:l + 1, :]).then_inc(s_prm, 16)
                sp.dma_start(taps[LNB:LNB + 1, :], A["ln_b"][l:l + 1, :]).then_inc(s_prm, 16)
                sp.dma_start(taps[STAP:NCH, :], A["w_sc"][l]).then_inc(s_prm, 16)
                for name, r, n in (("g_mix", 0, DC8), ("g_ffn", DC8, DC8), ("pool_scale", 2 * DC8, CP)):
                    sp.dma_start(urows[r:r + n, 1, l * P:(l + 1) * P],
                                 A[name][l].rearrange("(c p) -> c p", p=P)).then_inc(s_prm, 16)
            load_w_in(0, 0)
            load_w_in(0, 1)
            load_keys(0)
            load_w(w_out, "w_out", 0, s_wo)
            sp.wait_ge(s_wpz, 1)
            for l in range(DEPTH):
                for g in range(len(WINDOWS)):
                    r = 64 * (g % 2)
                    sp.dma_start(w_pool[r:r + 64, l, g // 2, r:r + 64], A["w_pool"][l, g]).then_inc(s_wp, 16)
            load_w(w_q, "w_q", 0, s_wq)
            sp.dma_start(g_fin[:, :], A["g_final"].rearrange("(a d) -> a d", a=1).partition_broadcast(P))\
                .then_inc(s_gfin, 16)
            mixer_io(0)
            for n in range(ITEMS):
                superstep_start(n)
                if n + 1 < ITEMS:
                    mixer_io(n + 1)
            superstep_start(ITEMS)
            store_out(ITEMS - 1)
            sp.wait_ge(s_xost, 16 * ITEMS)
            sp.wait_ge(s_nso, 48 * state_count(ITEMS - 1))
            sp.wait_ge(s_xst, 16 * ITEMS)

        @block.gpsimd
        def _(pool):
            nc.gpsimd.memset(ident[:, :], 0.0).then_inc(s_go, 1)
            nc.gpsimd.iota(iota_i[:, :], pattern=[[1, TOPK]], base=0, channel_multiplier=0).then_inc(s_const, 1)
            nc.gpsimd.memset(w_pool[:, :, :, :], 0.0).then_inc(s_wpz, 1)
            pool.wait_ge(s_go, 1)
            nc.gpsimd.affine_select(out=ident[:, :], in_=ident[:, :], compare_op=ALU.not_equal, fill=1.0,
                                    base=0, pattern=[[-1, P]], channel_multiplier=1).then_inc(s_const, 1)

            def fetch(rows, table, idx, j, src, t, free, staged, landed):
                item, group, n_before = src
                pool.wait_ge(free, (t + n_before) * RING + j + 1)
                nc.gpsimd.tensor_copy(idx[:, j:j + 1], ids[:, item % 3, bass.ds(t * RING + (group * RING + j), 1)])\
                    .then_inc(staged, 1)
                pool.wait_ge(staged, (t + n_before) * RING + j + 1)
                pool.sem_inc(s_go, 1)
                nc.gpsimd.indirect_dma_start(
                    out=rows[:, j, :], out_offset=None, in_=table[:, :],
                    in_offset=bass.IndirectOffsetOnAxis(ap=idx[:, j:j + 1], axis=0)).then_inc(landed[j], 16)

            def gather(t, u, v):
                for j in range(RING):
                    if u:
                        fetch(urows, eu, idx_u, j, u, t, s_ufree, s_ustg, s_urow)
                    if v:
                        fetch(vrows, ev, idx_v, j, v, t, s_vfree, s_vstg, s_vrow)

            for n in range(ITEMS + 1):
                if n < ITEMS:
                    pool.wait_ge(s_ids, n + 1)
                for part in range(PARTS):
                    run_part(pool, n, part, gather)

        @block.scalar
        def _(act):
            steps = [0]

            def step(ins):
                ins.then_inc(act_step, 1)
                steps[0] += 1

            def settle():
                act.wait_ge(act_step, steps[0])

            def rms_std(src, out, rows, done):
                step(nc.scalar.activation(psA[0:rows, :], src, ACT.Square, accum_out=stat[0:rows, out:out + 1]))
                settle()
                nc.scalar.activation(stat[0:rows, out + 1:out + 2], stat[0:rows, out:out + 1], ACT.Sqrt,
                                     bias=eps[0:rows, :], scale=1.0 / D).then_inc(done, 1)

            def mixer(m, part):
                l = m // TILES
                L = width(m)
                if part == 1:
                    act.wait_ge(s_x, 16 * sum(loads(i) for i in range(m + 1)))
                    if m == 0:
                        act.wait_ge(s_prmS, 2)
                    else:
                        act.wait_ge(s_qT, 2 * m)
                    rms_std(x_mix[:, :], 0, P, s_std1)
                    if m % TILES == 0:
                        act.wait_ge(s_ktT, l + 1)
                        nc.scalar.copy(keysT[:, :, :], psC[:, :].rearrange("p (h n) -> p h n", h=HEADS))\
                            .then_inc(s_kT, 1)
                if part == 4:
                    act.wait_ge(s_proj, 4 * m + 1)
                    act.wait_ge(s_t1, m + 1)
                    nc.scalar.activation(sig[:, :, 0:L], p_gate[:, :, 0:L], ACT.Sigmoid).then_inc(s_sig, 1)
                if part == 6:
                    act.wait_ge(s_proj, 4 * m + 3)
                    nc.scalar.copy(shc[:, :, 0:L], p_sh[:, :, 0:L]).then_inc(s_sh, 1)
                    act.wait_ge(s_d, m + 1)
                    nc.scalar.activation(sig[:, :, 0:L], zc[:, :, 0:L], ACT.Square).then_inc(s_sq, 1)
                if part == 7:
                    act.wait_ge(s_var, m + 1)
                    nc.scalar.activation(lnstd[:, 0:L], psB[:, 512:512 + L], ACT.Sqrt, bias=eps[:, :],
                                         scale=1.0 / DC).then_inc(s_lstd, 1)
                    act.wait_ge(s_ya, m + 1)
                    for c in range(CP):
                        if c == 0 and m:
                            act.wait_ge(s_sc, 2 * m)
                        step(nc.scalar.activation(yT[:, c, 0:L], psC[:, c * P:c * P + L], ACT.Copy,
                                                  scale=gain[:, l, 2 * DC8 + c:2 * DC8 + c + 1]))
                    act.wait_ge(s_xhat, m + 1)
                    for c in range(CC):
                        step(nc.scalar.activation(yT[:, CP + c, 0:L], zc[:, c, 0:L], ACT.Silu,
                                                  bias=chan[:, l, c, LNB:LNB + 1], scale=chan[:, l, c, LNG:LNG + 1]))
                    settle()
                    act.sem_inc(s_yab, 1)
                if part == 10:
                    act.wait_ge(s_x1, m + 1)
                    rms_std(x_mix[:, :], 2, P, s_std2)
                if part == 11:
                    act.wait_ge(s_bt, m + 1)
                    act.wait_ge(s_xst, 16 * (m + 1))
                    step(nc.scalar.copy(x_mix[:, :], psC[:, :]))
                    settle()
                    act.sem_inc(s_h, 1)
                if part in (11, 12):
                    q = part - 11
                    act.wait_ge(s_q, 2 * m + q + 1)
                    nc.scalar.copy(qT[:, 4 * q:4 * q + 4, :],
                                   psA[:, 512 * q:512 * q + 512].rearrange("p (h t) -> p h t", t=P))\
                        .then_inc(s_qT, 1)
                if part == 15:
                    act.wait_ge(s_e, m + 1)
                    nc.scalar.activation(best[:, :], best[:, :], ACT.Exp).then_inc(s_exp, 1)

            def superstep_start(n):
                if n >= 1:
                    act.wait_ge(s_dots, before(n) + 1)
                    k = groups(n - 1) * RING
                    nc.scalar.activation(gelu[:, 0:k], dots[:, 0:k], ACT.Gelu).then_inc(s_gelu, 1)
                if n < ITEMS:
                    if n >= 1:
                        act.wait_ge(s_ufree, (before(n) + 1) * RING)
                    act.wait_ge(s_h, n + 1)
                    nc.scalar.copy(h_cur[:, :], x_mix[:, :]).then_inc(s_hcur, 1)

            def final_std(v):
                if v >= TILES:
                    act.wait_ge(s_yend, v + 1)
                    if v + 1 < ITEMS:
                        act.wait_ge(s_qT, 2 * min(v + 3, ITEMS))
                    rms_std(x_out[0:width(v), :], 4, width(v), s_fstd)

            def weights(t, u, v):
                item, group, n_before = v
                act.wait_ge(s_diag, (t + n_before) * RING + 1)
                nc.scalar.copy(coef4[:, :], coef[:, ds4(t, group * RING)]).then_inc(s_coef4, 1)
                act.wait_ge(s_coef4, t + n_before + 1)
                for j in range(RING):
                    act.wait_ge(s_vfree, (t + n_before) * RING + j + 1)
                    nc.scalar.activation(diag[:, j, :], (fold if is_sample(item) else ident)[:, :], ACT.Copy,
                                         scale=coef4[:, j:j + 1]).then_inc(s_diag, 1)

            act.sem_inc(s_diag, 1)
            act.wait_ge(s_zero, 1)
            for part in range(PARTS):
                mixer(0, part)
            act.wait_ge(s_fold, 1)
            for n in range(ITEMS + 1):
                superstep_start(n)
                if n >= 2:
                    final_std(n - 2)
                if n >= 1:
                    act.wait_ge(s_coef, n)
                for part in range(PARTS):
                    if n + 1 < ITEMS:
                        mixer(n + 1, part)
                    run_part(act, n, part, weights, "v")
            final_std(ITEMS - 1)

        @block.tensor
        def _(pe):
            def turn(out, in_, rows=P):
                return nc.tensor.transpose(out, in_, ident[0:rows, 0:rows])

            def params():
                pe.wait_ge(s_const, 2)
                pe.wait_ge(s_prm, 16 * 8 * DEPTH)
                for l in range(DEPTH):
                    for c in range(CC):
                        o = (l * CC + c) * 64
                        turn(psB[:, o:o + NCH], urows[0:NCH, 0, l * DC + c * P:l * DC + (c + 1) * P], NCH)
                for l in range(DEPTH):
                    n = 2 * DC8 + CP
                    last = turn(psC[:, l * 64:l * 64 + n], urows[0:n, 1, l * P:(l + 1) * P], n)
                last.then_inc(s_prmT, 1)

            def queries(m, q):
                for h in range(4 * q, 4 * q + 4):
                    for c in range(DC8):
                        last = nc.tensor.matmul(psA[:, h * P:(h + 1) * P], w_q[:, c, h * P:(h + 1) * P],
                                                hT[:, c, :], start=c == 0, stop=c == DC8 - 1)
                last.then_inc(s_q, 1)

            def scores(m, q):
                pe.wait_ge(s_qT, 2 * m + q + 1)
                dst = psC if q else psB
                for h in range(4):
                    for half in range(2):
                        r = slice(half * DH, (half + 1) * DH)
                        o = 512 * half + NK * h
                        last = nc.tensor.matmul(dst[:, o:o + NK], qT[r, 4 * q + h, :], keysT[r, 4 * q + h, :],
                                                start=True, stop=True)
                last.then_inc(s_sc, 1)

            def mixer(m, part):
                l = m // TILES
                L = width(m)
                if part == 1:
                    if m % TILES == 0:
                        pe.wait_ge(s_kst, 16 * (l + 1))
                        if m:
                            pe.wait_ge(s_ids, m)
                        else:
                            pe.wait_ge(s_prmS, 2)
                        for h in range(HEADS):
                            last = turn(psC[:, h * P:(h + 1) * P], upper[:, h * P:(h + 1) * P])
                        last.then_inc(s_ktT, 1)
                    if is_sample(m):
                        pe.wait_ge(s_hst, 48 * (l + 1))
                        pe.wait_ge(s_ids, m)
                        for i, (_, _, rows) in enumerate(STATE_CHUNKS):
                            last = turn(psC[:, i * 32:i * 32 + rows], upper[0:rows, i * P:(i + 1) * P], rows)
                        last.then_inc(s_hstT, 1)
                    pe.wait_ge(s_xn, m + 1)
                    for c in range(DC8):
                        last = turn(psA[:, c * P:(c + 1) * P], xn[:, c * P:(c + 1) * P])
                    last.then_inc(s_t1, 1)
                if part in PROJ_PARTS:
                    if part == 2:
                        pe.wait_ge(s_hT, m + 1)
                        pe.wait_ge(s_wi[0], 16 * (l + 1))
                        if m:
                            pe.wait_ge(s_ids, m)
                    if part == 3:
                        if is_sample(m):
                            pe.wait_ge(s_hist, l + 1)
                        pe.wait_ge(s_kT, l + 1)
                    if part == 4:
                        pe.wait_ge(s_wi[1], 16 * (l + 1))
                    for col, dst, c in PROJ_PARTS[part]:
                        for k in range(DC8):
                            last = nc.tensor.matmul(dst[:, c, 0:L], w_in[:, k, col:col + P], hT[:, k, 0:L],
                                                    start=k == 0, stop=k == DC8 - 1)
                    last.then_inc(s_proj, 1)
                if part == 6:
                    pe.wait_ge(s_zc, m + 1)
                    for c in range(CC):
                        last = nc.tensor.matmul(psB[:, 0:L], ones[:, :], zc[:, c, 0:L],
                                                start=c == 0, stop=c == CC - 1)
                    last.then_inc(s_mean, 1)
                    pe.wait_ge(s_sq, m + 1)
                    for c in range(CC):
                        last = nc.tensor.matmul(psB[:, 512:512 + L], ones[:, :], sig[:, c, 0:L],
                                                start=c == 0, stop=c == CC - 1)
                    last.then_inc(s_var, 1)
                if part == 7:
                    pe.wait_ge(s_wp, 16 * DEPTH * len(WINDOWS))
                    pe.wait_ge(s_pd, m + 1)
                    for c in range(CP):
                        last = nc.tensor.matmul(psC[:, c * P:c * P + L], w_pool[:, l, c, :], pdif[:, c, 0:L],
                                                start=True, stop=True)
                    last.then_inc(s_ya, 1)
                if part == 8:
                    pe.wait_ge(s_yab, m + 1)
                    pe.wait_ge(s_yc, m + 1)
                    if outputs_state(m):
                        for i, (buf, c, rows) in enumerate(STATE_CHUNKS):
                            last = turn(psC[0:rows, i * P:(i + 1) * P], buf[:, c, L:L + rows])
                        last.then_inc(s_nst, 1)
                    pe.wait_ge(s_wo, 16 * (l + 1))
                if part in (8, 9):
                    half = slice(512 * (part - 8), 512 * (part - 7))
                    for c in range(DC8):
                        last = nc.tensor.matmul(psA[:, half], yT[:, c, :], w_out[:, c, half],
                                                start=c == 0, stop=c == DC8 - 1)
                    if part == 9:
                        last.then_inc(s_wod, 1)
                if part == 10:
                    pe.wait_ge(s_xn2, m + 1)
                    for c in range(DC8):
                        last = turn(psB[:, c * P:(c + 1) * P], xn[:, c * P:(c + 1) * P])
                    last.then_inc(s_t2, 1)
                if part == 11:
                    pe.wait_ge(s_hT2, m + 1)
                    if outputs_state(m):
                        pe.wait_ge(s_nsc, state_count(m))
                    for c in range(DC8):
                        last = turn(psC[:, c * P:(c + 1) * P], hT[:, c, :])
                    last.then_inc(s_bt, 1)
                    pe.wait_ge(s_wq, 16 * (l + 1))
                    queries(m, 0)
                    scores(m, 0)
                if part == 12:
                    queries(m, 1)
                    pe.wait_ge(s_h, m + 1)
                    scores(m, 1)

            def clear(start):
                for half in (0, 512):
                    last = nc.tensor.matmul(yacc[:, half:half + 512], zeros[:, 0:P], zeros[:, :],
                                            start=start, stop=not start, skip_group_check=True)
                return last

            def add_rows(t, u, v):
                n_before = v[2]
                for j in range(RING):
                    pe.wait_ge(s_vrow[j], (t + n_before) * 16 + 16)
                    pe.wait_ge(s_diag, (t + n_before) * RING + j + 2)
                    for half in (0, 512):
                        last = nc.tensor.matmul(yacc[:, half:half + 512], diag[:, j, :],
                                                vrows[:, j, half:half + 512], start=False, stop=False,
                                                skip_group_check=True)
                    last.then_inc(s_vfree, 1)

            pe.sem_inc(s_vfree, RING)
            params()
            for part in range(PARTS):
                mixer(0, part)
            pe.wait_ge(s_zero, 1)
            for n in range(ITEMS + 1):
                if n >= 1:
                    if n >= 2:
                        pe.wait_ge(s_yend, n - 1)
                    clear(True)
                for part in range(PARTS):
                    if n + 1 < ITEMS:
                        mixer(n + 1, part)
                    run_part(pe, n, part, add_rows, "v")
                if n >= 1:
                    clear(False).then_inc(s_ysum, 1)

        @block.vector
        def _(dve):
            steps = [0]

            def step(ins):
                ins.then_inc(dve_step, 1)
                steps[0] += 1

            def settle(back=0):
                if steps[0] > back:
                    dve.wait_ge(dve_step, steps[0] - back)

            def chain(ins):
                step(ins)
                settle()

            def consts():
                nc.vector.memset(eps[:, :], EPS)
                nc.vector.memset(ones[:, :], 1.0)
                nc.vector.memset(zeros[:, :], 0.0)
                chain(nc.vector.memset(stat[:, :], 0.0))
                dve.sem_inc(s_zero, 1)
                dve.wait_ge(s_const, 2)
                for q in range(COPIES):
                    r = slice(q * LS, (q + 1) * LS)
                    step(nc.vector.tensor_copy(
                        fold[r, :].rearrange("p (q t) -> p q t", q=COPIES),
                        ident[r, r].unsqueeze(1).to_broadcast([LS, COPIES, LS])))
                chain(nc.vector.tensor_copy(iota_f[:, :], iota_i[:, :]))
                dve.sem_inc(s_fold, 1)
                for g, w in enumerate(WINDOWS):
                    r = slice(64 * (g % 2), 64 * (g % 2) + 64)
                    step(nc.vector.tensor_scalar(rcnt[r, g // 2, :], iota_f[r, :], 1.0, float(w), ALU.add, ALU.min))
                settle()
                chain(nc.vector.reciprocal(rcnt[:, :, :], rcnt[:, :, :]))
                dve.wait_ge(s_prmT, 1)
                nc.vector.tensor_copy(
                    chan[:, :, :, :].rearrange("p l c r -> p (l c) r"),
                    psB[:, 0:DEPTH * CC * 64].rearrange("p (g r) -> p g r", r=64)[:, :, 0:NCH]).then_inc(s_prmS, 1)
                nc.vector.tensor_copy(
                    gain[:, :, :],
                    psC[:, 0:DEPTH * 64].rearrange("p (g r) -> p g r", r=64)[:, :, 0:2 * DC8 + CP])\
                    .then_inc(s_prmS, 1)
                dve.wait_ge(s_prmS, 2)

            def norm(src, col, out, rows=P):
                chain(nc.vector.reciprocal(stat[0:rows, col + 1:col + 2], stat[0:rows, col + 1:col + 2]))
                return nc.vector.tensor_scalar(out, src, stat[0:rows, col + 1:col + 2], None, ALU.mult)

            def scale_turned(ps_src, l, first):
                return nc.vector.tensor_tensor(
                    hT[:, :, :], ps_src[:, :].rearrange("p (c t) -> p c t", t=P),
                    gain[:, l, first:first + DC8].unsqueeze(2).to_broadcast([P, DC8, P]), ALU.mult)

            def taps(m, lo, hi):
                l, L = m // TILES, width(m)
                for k in range(lo, hi):
                    for c in range(CC):
                        z = zbuf[:, c, k:k + L]
                        w = chan[:, l, c, k:k + 1]
                        settle(CC - 1 if k else 0)
                        if k == 0:
                            step(nc.vector.tensor_scalar(zc[:, c, 0:L], z, w, chan[:, l, c, BIAS:BIAS + 1],
                                                         ALU.mult, ALU.add))
                        else:
                            step(nc.vector.scalar_tensor_tensor(out=zc[:, c, 0:L], in0=z, scalar=w,
                                                                in1=zc[:, c, 0:L], op0=ALU.mult, op1=ALU.add))

            def histories(m, which):
                for i, (buf, h) in enumerate(((ubuf, HP), (zbuf, HC), (mbuf, HS))):
                    if i not in which:
                        continue
                    if m % TILES == 0:
                        chain(nc.vector.memset(buf[:, :, 0:h], 0.0))
                    elif not is_sample(m):
                        chain(nc.vector.tensor_copy(buf[:, :, 0:h], buf[:, :, P:P + h]))

            def pool_windows(m):
                L = width(m)
                E = HP + L
                dve.wait_ge(s_proj, 4 * m + 2)
                chain(nc.vector.tensor_copy(ubuf[:, :, HP:E], p_u[:, :, 0:L]))
                chain(nc.vector.tensor_tensor(win_a[:, :, 1:E], ubuf[:, :, 1:E], ubuf[:, :, 0:E - 1], ALU.add))
                chain(nc.vector.tensor_tensor(win_b[:, :, 3:E], win_a[:, :, 3:E], win_a[:, :, 1:E - 2], ALU.add))
                chain(nc.vector.tensor_tensor(win_a[:, 1, 7:E], win_b[:, 1, 7:E], win_b[:, 1, 3:E - 4], ALU.add))
                chain(nc.vector.tensor_tensor(win_b[64:128, 1, 15:E], win_a[64:128, 1, 15:E],
                                              win_a[64:128, 1, 7:E - 8], ALU.add))
                sums = (win_a, win_b, win_a, win_b)
                for g, w in enumerate(WINDOWS):
                    r, c = slice(64 * (g % 2), 64 * (g % 2) + 64), g // 2
                    step(nc.vector.scalar_tensor_tensor(
                        out=pdif[r, c, 0:L], in0=sums[g][r, c, HP:E], scalar=1.0 / w,
                        in1=ubuf[r, c, HP:E], op0=ALU.mult, op1=ALU.subtract))
                settle()
                if m % TILES == 0:
                    for g in range(len(WINDOWS)):
                        r, c = slice(64 * (g % 2), 64 * (g % 2) + 64), g // 2
                        step(nc.vector.tensor_tensor(pdif[r, c, 0:TOPK], sums[g][r, c, HP:HP + TOPK],
                                                     rcnt[r, c, :], ALU.mult))
                    settle()
                    chain(nc.vector.tensor_tensor(pdif[:, :, 0:TOPK], pdif[:, :, 0:TOPK],
                                                  ubuf[:, :, HP:HP + TOPK], ALU.subtract))
                dve.sem_inc(s_pd, 1)

            def short_conv(m):
                l, L = m // TILES, width(m)
                dve.wait_ge(s_sh, m + 1)
                dve.wait_ge(s_proj, 4 * m + 4)
                if m:
                    dve.wait_ge(s_sc, 2 * m)
                chain(nc.vector.tensor_tensor(mbuf[:, :, HS:HS + L], p_sc[:, :, 0:L], shc[:, :, 0:L], ALU.mult))
                for k in range(HS + 1):
                    for c in range(CS):
                        x, w = mbuf[:, c, k:k + L], chan[:, l, c, STAP + k:STAP + k + 1]
                        settle(CS - 1 if k else 0)
                        if k == 0:
                            step(nc.vector.tensor_scalar(shc[:, c, 0:L], x, w, None, ALU.mult))
                        else:
                            step(nc.vector.scalar_tensor_tensor(out=shc[:, c, 0:L], in0=x, scalar=w,
                                                                in1=shc[:, c, 0:L], op0=ALU.mult, op1=ALU.add))
                settle()
                step(nc.vector.tensor_tensor(yT[:, CP + CC:DC8, 0:L], p_sb[:, :, 0:L], shc[:, :, 0:L], ALU.mult))
                settle()
                if not is_sample(m):
                    dve.sem_inc(s_yc, 1)

            def top16(values, scratch, out_v, out_i):
                chain(nc.vector.max(out_v[:, 0:8], values))
                step(nc.vector.max_index(out_i[:, 0:8], out_v[:, 0:8], values))
                chain(nc.vector.match_replace(scratch, out_v[:, 0:8], values, LOWEST))
                chain(nc.vector.max(out_v[:, 8:16], scratch))
                chain(nc.vector.max_index(out_i[:, 8:16], out_v[:, 8:16], scratch))

            def route(m, pair):
                q = pair // 2
                src = psC if q else psB
                dve.wait_ge(s_sc, 2 * m + q + 1)
                if pair == 0 and outputs_state(m):
                    dve.wait_ge(s_nso, 48 * state_count(m))
                for h in range(2):
                    for half in range(2):
                        o = 512 * half + NK * (2 * (pair % 2) + h)
                        top16(src[:, o:o + NK], wk128, tv[:, h, half, :], ti[:, h, half, :])
                step(nc.vector.tensor_copy(tif[:, :, :, :], ti[:, :, :, :]))
                for h in range(2):
                    step(nc.vector.tensor_tensor(
                        cand[:, h, :, :], tv[:, h, 0, :].unsqueeze(2).to_broadcast([P, TOPK, TOPK]),
                        tv[:, h, 1, :].unsqueeze(1).to_broadcast([P, TOPK, TOPK]), ALU.add))
                settle()
                for h in range(2):
                    b = best[:, (2 * pair + h) * TOPK:(2 * pair + h + 1) * TOPK]
                    top16(cand[:, h, :, :].rearrange("p a b -> p (a b)"), wk256, b, bj[:, h, :])
                step(nc.vector.tensor_scalar(ab[:, 0, :, :], bj[:, :, :], 4, None, ALU.logical_shift_right))
                step(nc.vector.tensor_scalar(ab[:, 1, :, :], bj[:, :, :], TOPK - 1, None, ALU.bitwise_and))
                settle()
                chain(nc.vector.tensor_copy(abf[:, :, :, :], ab[:, :, :, :]))
                for half in range(2):
                    chain(nc.vector.tensor_tensor(
                        onehot[:, :, :, :], abf[:, half, :, :].unsqueeze(3).to_broadcast([P, 2, TOPK, TOPK]),
                        iota_f[:, :].unsqueeze(1).unsqueeze(1).to_broadcast([P, 2, TOPK, TOPK]), ALU.is_equal))
                    chain(nc.vector.tensor_tensor(
                        onehot[:, :, :, :], onehot[:, :, :, :],
                        tif[:, :, half, :].unsqueeze(2).to_broadcast([P, 2, TOPK, TOPK]), ALU.mult))
                    chain(nc.vector.tensor_reduce(ij[:, half, :, :], onehot[:, :, :, :], AX.X, ALU.add))
                o = 2 * pair * TOPK
                chain(nc.vector.scalar_tensor_tensor(
                    out=idf[:, o:o + 2 * TOPK], in0=ij[:, 0, :, :].rearrange("p h k -> p (h k)"),
                    scalar=float(NK), in1=ij[:, 1, :, :].rearrange("p h k -> p (h k)"),
                    op0=ALU.mult, op1=ALU.add))

            def finish_routing(m):
                b3 = best[:, :].rearrange("p (h k) -> p h k", k=TOPK)
                chain(nc.vector.tensor_copy(hsum[:, :], b3[:, :, 0]))
                chain(nc.vector.tensor_tensor(b3, b3, hsum[:, :].unsqueeze(2).to_broadcast([P, HEADS, TOPK]),
                                              ALU.subtract))
                dve.sem_inc(s_e, 1)
                base = float(m // TILES * NE)
                spans = [(slice(q * LS, (q + 1) * LS), slice(q * 32, q * 32 + 32)) for q in range(COPIES)] \
                    if is_sample(m) else [(slice(0, P), slice(0, KPICK))]
                for r, cols in spans:
                    n = cols.stop - cols.start
                    step(nc.vector.tensor_scalar(ids[r, m % 3, 0:n], idf[r, cols], base, None, ALU.add))
                dve.wait_ge(s_exp, m + 1)
                chain(nc.vector.tensor_reduce(hsum[:, :], b3, AX.X, ALU.add))
                chain(nc.vector.reciprocal(hsum[:, :], hsum[:, :]))
                chain(nc.vector.tensor_tensor(b3, b3, hsum[:, :].unsqueeze(2).to_broadcast([P, HEADS, TOPK]),
                                              ALU.mult))
                for r, cols in spans:
                    n = cols.stop - cols.start
                    step(nc.vector.tensor_copy(gates[r, m % 2, 0:n], best[r, cols]))
                settle()
                dve.sem_inc(s_ids, 1)

            def mixer(m, part):
                l, L = m // TILES, width(m)
                if part == 1:
                    dve.wait_ge(s_std1, m + 1)
                    norm(x_mix[:, :], 0, xn).then_inc(s_xn, 1)
                    if is_sample(m):
                        dve.wait_ge(s_hstT, l + 1)
                        ph = psC[:, 0:256].rearrange("p (i t) -> p i t", t=32)
                        step(nc.vector.tensor_copy(ubuf[:, :, 0:HP], ph[:, 0:CP, 0:HP]))
                        step(nc.vector.tensor_copy(zbuf[:, :, 0:HC], ph[:, CP:CP + CC, 0:HC]))
                        step(nc.vector.tensor_copy(mbuf[:, :, 0:HS], ph[:, CP + CC:DC8, 0:HS]))
                        settle()
                        dve.sem_inc(s_hist, 1)
                    dve.wait_ge(s_t1, m + 1)
                    scale_turned(psA, l, 0).then_inc(s_hT, 1)
                if part == 4:
                    histories(m, (1,))
                    dve.wait_ge(s_sig, m + 1)
                    dve.wait_ge(s_proj, 4 * m + 2)
                    chain(nc.vector.tensor_tensor(zbuf[:, :, HC:HC + L], p_val[:, :, 0:L], sig[:, :, 0:L], ALU.mult))
                    taps(m, 0, HC // 2)
                if part == 5:
                    taps(m, HC // 2, HC + 1)
                    settle()
                    dve.sem_inc(s_zc, 1)
                if part == 6:
                    dve.wait_ge(s_mean, m + 1)
                    nc.vector.scalar_tensor_tensor(
                        out=zc[:, :, 0:L], in0=psB[:, 0:L].unsqueeze(1).to_broadcast([P, CC, L]),
                        scalar=-1.0 / DC, in1=zc[:, :, 0:L], op0=ALU.mult, op1=ALU.add).then_inc(s_d, 1)
                    histories(m, (0, 2))
                    pool_windows(m)
                    short_conv(m)
                if part == 7:
                    dve.wait_ge(s_lstd, m + 1)
                    chain(nc.vector.reciprocal(lnstd[:, 0:L], lnstd[:, 0:L]))
                    nc.vector.tensor_tensor(zc[:, :, 0:L], zc[:, :, 0:L],
                                            lnstd[:, 0:L].unsqueeze(1).to_broadcast([P, CC, L]), ALU.mult)\
                        .then_inc(s_xhat, 1)
                    if is_sample(m):
                        dve.wait_ge(s_yab, m + 1)
                        chain(nc.vector.tensor_copy(
                            yT[:, :, L:P].rearrange("p c (q t) -> p c q t", t=L),
                            yT[:, :, 0:L].unsqueeze(2).to_broadcast([P, DC8, COPIES - 1, L])))
                        dve.sem_inc(s_yc, 1)
                if part == 9 and outputs_state(m):
                    dve.wait_ge(s_nst, state_count(m))
                    for rows, cols in ((HP, slice(0, DP)), (HC, slice(DP, DP + DC)), (HS, slice(DP + DC, D))):
                        step(nc.vector.tensor_copy(upper[0:rows, cols], psC[0:rows, cols]))
                    settle()
                    dve.sem_inc(s_nsc, 1)
                if part == 10:
                    dve.wait_ge(s_wod, m + 1)
                    nc.vector.tensor_tensor(x_mix[:, :], psA[:, :], x_mix[:, :], ALU.add).then_inc(s_x1, 1)
                    dve.wait_ge(s_std2, m + 1)
                    norm(x_mix[:, :], 2, xn).then_inc(s_xn2, 1)
                if part == 11:
                    dve.wait_ge(s_t2, m + 1)
                    scale_turned(psB, l, DC8).then_inc(s_hT2, 1)
                if part >= 12:
                    route(m, part - 12)
                if part == 15:
                    finish_routing(m)

            def take_sums(v):
                rows = width(v)
                dve.wait_ge(s_ysum, v + 1)
                dve.wait_ge(s_xo, 16 * (v + 1))
                nc.vector.tensor_tensor(x_out[0:rows, :], yacc[0:rows, :], x_out[0:rows, :], ALU.add)\
                    .then_inc(s_yend, 1)

            def final_norm(v):
                rows = width(v)
                dve.wait_ge(s_gfin, 16)
                dve.wait_ge(s_fstd, v - TILES + 1)
                chain(norm(x_out[0:rows, :], 4, x_out[0:rows, :], rows))
                nc.vector.tensor_tensor(x_out[0:rows, :], x_out[0:rows, :], g_fin[0:rows, :], ALU.mult)\
                    .then_inc(s_fin, 1)

            def dot_rows(t, u, v):
                item, group, n_before = u
                dve.wait_ge(s_dots, t + n_before + 1)
                for j in range(RING):
                    dve.wait_ge(s_urow[j], (t + n_before) * 16 + 16)
                    nc.vector.tensor_tensor_reduce(urows[:, j, :], urows[:, j, :], h_cur[:, :], 1.0, 0.0,
                                                   ALU.mult, ALU.add, dots4[:, j:j + 1]).then_inc(s_ufree, 1)
                dve.wait_ge(s_ufree, (t + n_before) * RING + 2 * RING)
                nc.vector.tensor_copy(dots[:, ds4(t, group * RING)], dots4[:, :]).then_inc(s_dots, 1)

            dve.sem_inc(s_ufree, RING)
            dve.sem_inc(s_dots, 1)
            consts()
            for part in range(PARTS):
                mixer(0, part)
            for n in range(ITEMS + 1):
                if n >= 2:
                    take_sums(n - 2)
                if n >= 1:
                    k = groups(n - 1) * RING
                    dve.wait_ge(s_gelu, n)
                    nc.vector.tensor_tensor(coef[:, 0:k], gelu[:, 0:k], gates[:, (n - 1) % 2, 0:k], ALU.mult)\
                        .then_inc(s_coef, 1)
                if n - 2 >= TILES:
                    final_norm(n - 2)
                if n < ITEMS:
                    dve.wait_ge(s_hcur, n + 1)
                for part in range(PARTS):
                    if n + 1 < ITEMS:
                        mixer(n + 1, part)
                    run_part(dve, n, part, dot_rows, "u")
            take_sums(ITEMS - 1)
            final_norm(ITEMS - 1)


_INS = ['x_prompt', 'x_sample', 'state_pool', 'state_dwconv', 'state_shortconv', 'g_mix', 'w_in', 'w_pool',
        'pool_scale', 'w_dw', 'b_dw', 'ln_g', 'ln_b', 'w_sc', 'w_out', 'g_ffn', 'w_q', 'sub_keys', 'expert_u',
        'expert_v', 'g_final']
_OUTS = ['y_prompt', 'y_sample', 'new_pool_prompt', 'new_dwconv_prompt', 'new_shortconv_prompt',
         'new_pool_sample', 'new_dwconv_sample', 'new_shortconv_sample']


def kernel(**inputs):
    import numpy as _np
    import concourse.bacc as _bacc
    from concourse import mybir as _mybir
    from concourse.bass_utils import run_bass_kernel_spmd as _run

    nc = _bacc.Bacc("TRN2", target_bir_lowering=False, num_devices=1, dynamic_dma_scratch_size=4096)
    arrays, ins, outs = {}, {}, {}
    for name in _INS:
        a = _np.ascontiguousarray(inputs[name])
        arrays[f"in_{name}"] = a
        ins[name] = nc.dram_tensor(f"in_{name}", a.shape, _mybir.dt.from_np(a.dtype), kind="ExternalInput").ap()
    shape = {n: inputs[n].shape for n in _INS}
    batch = shape['x_prompt'][0]
    out_shapes = [shape['x_prompt'], shape['x_sample']]
    for _ in range(2):
        out_shapes += [(s[0], batch) + tuple(s[2:]) for s in
                       (shape['state_pool'], shape['state_dwconv'], shape['state_shortconv'])]
    for name, s in zip(_OUTS, out_shapes):
        outs[name] = nc.dram_tensor(f"out_{name}", tuple(s), _mybir.dt.float32, kind="ExternalOutput").ap()
    build(nc, ins, outs)
    r = _run(nc, [arrays], core_ids=[0])
    return tuple(r.results[0][f"out_{name}"] for name in _OUTS)
```

```python
from contextlib import ExitStack

import concourse.bass as bass
from concourse import mybir

ALU = mybir.AluOpType
ACT = mybir.ActivationFunctionType
AX = mybir.AxisListType
F32 = mybir.dt.float32
BF16 = mybir.dt.bfloat16
U32 = mybir.dt.uint32
I32 = mybir.dt.int32

P = 128
RING = 4
TICKS = 32
EPS = 1e-6
LOWEST = -3.0e38


NORM, GATE_SIGMOID, CONV, POOLING, SHORT, W_OUT, NORM2, FFN_H, QUERY, ROUTE, FINISH = \
    1, 4, 5, 9, 10, 11, 15, 16, 16, 18, 30
PROJ_TICKS = {2: 3, 3: 2, 4: 3, 5: 2, 6: 3, 7: 2, 8: 2}
W_OUT_TICKS = QUERY_TICKS = CONV_TICKS = 4


def build(nc, A, O):
    DEPTH, D = A["g_mix"].shape
    SEQ, LS = A["x_prompt"].shape[1], A["x_sample"].shape[1]
    DP, DC, DSC = A["state_pool"].shape[3], A["state_dwconv"].shape[3], A["state_shortconv"].shape[3]
    HP, HC, HS = A["state_pool"].shape[2], A["state_dwconv"].shape[2], A["state_shortconv"].shape[2]
    NE = A["expert_u"].shape[1]
    HEADS, NK, DH = A["sub_keys"].shape[1], A["sub_keys"].shape[3], A["sub_keys"].shape[4]
    TOPK = 16
    KPICK = HEADS * TOPK
    DC8 = D // P
    CP, CC, CS = DP // P, DC // P, DSC // P
    D_IN = DP + 2 * DC + 3 * DSC
    WINDOWS = (2, 4, 8, 16)
    TILES = SEQ // P + 1
    ITEMS = DEPTH * TILES
    COPIES = P // LS
    assert (CP, CC, CS, DC8, KPICK, NK, DH, COPIES) == (2, 3, 3, 8, 128, 128, 64, 4)

    def is_sample(m):
        return m % TILES == TILES - 1

    def width(m):
        return LS if is_sample(m) else P

    def loads(m):
        return COPIES if is_sample(m) else 1

    def groups(m):
        return (KPICK // COPIES if is_sample(m) else KPICK) // RING

    def groups_by(m, tick):
        return tick * groups(m) // TICKS

    def before(m):
        return sum(groups(i) for i in range(m))

    def outputs_state(m):
        return m % TILES >= TILES - 2

    def state_count(m):
        return sum(outputs_state(i) for i in range(m + 1))

    eu = A["expert_u"].rearrange("l e d -> (l e) d")
    ev = A["expert_v"].rearrange("l e d -> (l e) d")

    with ExitStack() as ctx:
        def sb(name, shape, dt=F32):
            return ctx.enter_context(nc.sbuf_tensor(name, shape, dt))

        def ps(name):
            return ctx.enter_context(nc.psum_tensor(name, [P, 1024], F32))

        def sem(name):
            return ctx.enter_context(nc.semaphore(name))

        w_in = sb("w_in_sb", [P, DC8, D_IN])
        w_out = sb("w_out_sb", [P, DC8, D])
        w_q = sb("w_q_sb", [P, DC8, D])
        keysT = sb("keysT", [P, HEADS, NK])
        urows = sb("urows", [P, RING, D])
        vrows = sb("vrows", [P, RING, D])
        diag = sb("diag", [P, RING, P])
        h_cur = sb("h_cur", [P, D])
        x_mix = sb("x_mix", [P, D])
        x_out = sb("x_out", [P, D])
        g_fin = sb("g_fin", [P, D])
        hT = sb("hT", [P, DC8, P])
        yT = sb("yT", [P, DC8, P])
        qT = yT
        work = sb("work", [P, 2048])
        zbuf = sb("zbuf", [P, CC, HC + P])
        ubuf = sb("ubuf", [P, CP, HP + P])
        mbuf = sb("mbuf", [P, CS, HS + P])
        ids = sb("ids", [P, 3, KPICK], U32)
        gates = sb("gates", [P, 2, KPICK])
        dots = sb("dots", [P, KPICK])
        dots4 = sb("dots4", [P, RING])
        gelu = sb("gelu", [P, KPICK])
        coef = sb("coef", [P, KPICK])
        coef4 = sb("coef4", [P, RING])
        idf = sb("idf", [P, KPICK])
        best = sb("best", [P, KPICK])
        ident = sb("ident", [P, P])
        fold = sb("fold", [P, P])
        ones = sb("ones", [P, P])
        zeros = sb("zeros", [P, 512], BF16)
        w_pool = sb("w_pool_sb", [P, DEPTH, CP, P])
        chan = sb("chan", [P, DEPTH, CC, HC + 1 + 3 + HS + 1])
        gain = sb("gain", [P, DEPTH, 2 * DC8 + CP])
        stat = sb("stat", [P, 8])
        hsum = sb("hsum", [P, HEADS])
        iota_i = sb("iota_i", [P, TOPK], I32)
        iota_f = sb("iota_f", [P, TOPK])
        rcnt = sb("rcnt", [P, CP, TOPK])
        idx_u = sb("idx_u", [P, RING], U32)
        idx_v = sb("idx_v", [P, RING], U32)
        eps = sb("eps", [P, 1])
        x_mid = nc.dram_tensor("x_mid", [SEQ + LS, D], F32).ap()

        NCH = HC + 1 + 3 + HS + 1
        TAP, BIAS, LNG, LNB, STAP = 0, HC + 1, HC + 2, HC + 3, HC + 4

        xn = work[:, 0:1024]
        upper = work[:, 1024:2048]
        zc = work[:, 0:384].rearrange("p (c t) -> p c t", c=CC)
        sig = work[:, 384:768].rearrange("p (c t) -> p c t", c=CC)
        lnstd = work[:, 384:512]
        win_a = work[:, 768:768 + CP * (HP + P)].rearrange("p (c t) -> p c t", c=CP)
        win_b = work[:, 1056:1056 + CP * (HP + P)].rearrange("p (c t) -> p c t", c=CP)
        pdif = work[:, 1344:1600].rearrange("p (c t) -> p c t", c=CP)
        shc = work[:, 1600:1984].rearrange("p (c t) -> p c t", c=CS)
        cand = work[:, 0:512].rearrange("p (h a b) -> p h a b", h=2, a=TOPK)
        wk256 = work[:, 512:768]
        onehot = work[:, 768:1280].rearrange("p (h s m) -> p h s m", h=2, s=TOPK)
        wk128 = work[:, 1280:1408]
        tv = work[:, 1408:1472].rearrange("p (h q k) -> p h q k", h=2, q=2)
        ti = work[:, 1472:1536].bitcast(U32).rearrange("p (h q k) -> p h q k", h=2, q=2)
        tif = work[:, 1536:1600].rearrange("p (h q k) -> p h q k", h=2, q=2)
        bj = work[:, 1600:1632].bitcast(U32).rearrange("p (h k) -> p h k", h=2)
        ab = work[:, 1632:1696].bitcast(U32).rearrange("p (q h k) -> p q h k", q=2, h=2)
        abf = work[:, 1696:1760].rearrange("p (q h k) -> p q h k", q=2, h=2)
        ij = work[:, 1760:1824].rearrange("p (q h k) -> p q h k", q=2, h=2)

        psA, psB, psC, yacc = ps("psA"), ps("psB"), ps("psC"), ps("yacc")

        def tri(ap):
            return ap.rearrange("p (c t) -> p c t", t=P)

        p_gate, p_val = tri(psB[:, 0:384]), tri(psB[:, 512:896])
        p_u, p_sh = tri(psC[:, 0:256]), tri(psC[:, 512:896])
        p_sc, p_sb = tri(psA[:, 0:384]), tri(psA[:, 512:896])
        PROJ = []
        for dst, first, n in ((p_gate, DP + DC, CC), (p_val, DP, CC), (p_u, 0, CP),
                              (p_sh, DP + 2 * DC, CS), (p_sc, DP + 2 * DC + 2 * DSC, CS),
                              (p_sb, DP + 2 * DC + DSC, CS)):
            PROJ += [(first + c * P, dst, c) for c in range(n)]
        proj_of, last_chunk = {}, []
        for tick, n in PROJ_TICKS.items():
            done = last_chunk[-1] if last_chunk else 0
            proj_of[tick] = PROJ[done:done + n]
            last_chunk.append(done + n)
        assert last_chunk[-1] == len(PROJ)

        def proj_count(m, chunks):
            return len(last_chunk) * m + 1 + min(i for i, n in enumerate(last_chunk) if n >= chunks)
        GATE, VAL = CC, 2 * CC
        U = VAL + CP
        SH, SC, SB = U + CS, U + 2 * CS, U + 3 * CS
        STATE_CHUNKS = [(ubuf, c, HP) for c in range(CP)] + [(zbuf, c, HC) for c in range(CC)] + \
                       [(mbuf, c, HS) for c in range(CS)]

        s_const = sem("consts_made")
        s_fold = sem("fold_made")
        s_zero = sem("zeros_made")
        s_prm = sem("params_loaded")
        s_prmT = sem("params_turned")
        s_prmS = sem("params_stored")
        s_gfin = sem("g_final_loaded")
        s_wpz = sem("w_pool_cleared")
        s_wp = sem("w_pool_loaded")
        s_wi = [sem("w_in_loaded_a"), sem("w_in_loaded_b")]
        s_wo = sem("w_out_loaded")
        s_wq = sem("w_q_loaded")
        s_kst = sem("keys_loaded")
        s_ktT = sem("keys_turned")
        s_kT = sem("keys_stored")
        s_hst = sem("states_loaded")
        s_hstT = sem("states_turned")
        s_hist = sem("histories_set")
        s_x = sem("x_loaded")
        s_std1 = sem("x_std")
        s_xn = sem("x_normed")
        s_t1 = sem("x_turned")
        s_hT = sem("hT_set")
        s_proj = sem("projected")
        s_sig = sem("gate_sigmoid")
        s_zc = sem("conv_done")
        s_mean = sem("ln_sum")
        s_d = sem("ln_centred")
        s_sq = sem("ln_squared")
        s_var = sem("ln_sum_sq")
        s_lstd = sem("ln_std")
        s_xhat = sem("ln_normed")
        s_pd = sem("pool_diff")
        s_ya = sem("pool_mixed")
        s_sh = sem("s_h_copied")
        s_yab = sem("yT_pool_conf_set")
        s_yc = sem("yT_short_set")
        s_nst = sem("new_states_turned")
        s_nsc = sem("new_states_copied")
        s_nso = sem("new_states_stored")
        s_wod = sem("w_out_done")
        s_x1 = sem("x_mixed")
        s_xst = sem("x_mixed_stored")
        s_std2 = sem("x1_std")
        s_xn2 = sem("x1_normed")
        s_t2 = sem("x1_turned")
        s_hT2 = sem("ffn_hT_set")
        s_bt = sem("h_turned_back")
        s_h = sem("h_set")
        s_q = sem("queries_made")
        s_qT = sem("queries_copied")
        s_sc = sem("scores_made")
        s_e = sem("gate_logits")
        s_exp = sem("gate_exp")
        s_ids = sem("ids_ready")
        s_hcur = sem("h_cur_set")
        s_dots = sem("dots_copied")
        s_gelu = sem("gelu_done")
        s_coef = sem("coef_ready")
        s_urow = [sem(f"u_row_landed_{j}") for j in range(RING)]
        s_vrow = [sem(f"v_row_landed_{j}") for j in range(RING)]
        s_ufree = sem("u_rows_free")
        s_vfree = sem("v_rows_free")
        s_ustg = sem("u_indices_staged")
        s_vstg = sem("v_indices_staged")
        s_go = sem("pool_goes_on")
        s_coef4 = sem("coef4_staged")
        s_diag = sem("diag_made")
        s_ysum = sem("v_rows_summed")
        s_xo = sem("x_out_loaded")
        s_yend = sem("x_out_added")
        s_fstd = sem("final_std")
        s_fin = sem("final_normed")
        s_xost = sem("x_out_stored")
        dve_step = sem("dve_step")
        act_step = sem("act_step")

        block = ctx.enter_context(nc.Block())

        def rows_of(m):
            k = m % TILES
            return slice(k * P, k * P + width(m))

        def x_source(m):
            if m >= TILES:
                return x_mid[rows_of(m), :]
            if is_sample(m):
                return A["x_sample"][0, :, :]
            return A["x_prompt"][0, m * P:(m + 1) * P, :]

        def gather_groups(eng, item, first, last, body):
            lo, hi = groups_by(item, first), groups_by(item, last)
            if hi - lo > 1:
                with eng.Fori(0, hi - lo) as t:
                    body(item, t + lo)
            elif hi > lo:
                body(item, lo)

        def superstep(eng, n, item, slices, mixer, body):
            cuts = sorted(t for t in set(slices) if n + 1 < ITEMS) + [TICKS]
            gathers = 0 <= item < ITEMS
            if gathers:
                gather_groups(eng, item, 0, cuts[0], body)
            for tick, upto in zip(cuts, cuts[1:]):
                mixer(n + 1, tick)
                if gathers:
                    gather_groups(eng, item, tick, upto, body)

        @block.sync
        def _(sp):
            def load_w_in(l, half):
                cols = slice(0, DP + 2 * DC) if half == 0 else slice(DP + 2 * DC, D_IN)
                sp.dma_start(w_in[:, :, cols], A["w_in"][l].rearrange("(c p) n -> p c n", p=P)[:, :, cols])\
                    .then_inc(s_wi[half], 16)

            def load_w(dst, name, l, s):
                sp.dma_start(dst[:, :, :], A[name][l].rearrange("(c p) n -> p c n", p=P)).then_inc(s, 16)

            def load_keys(l):
                sp.dma_start(upper.rearrange("p (h q d) -> p h q d", h=HEADS, q=2),
                             A["sub_keys"][l].rearrange("h q n d -> n h q d")).then_inc(s_kst, 16)

            def load_x(m):
                if m >= TILES:
                    sp.wait_ge(s_xost, 16 * (m - TILES + 1))
                for q in range(loads(m)):
                    rows = width(m)
                    sp.dma_start(x_mix[q * rows:(q + 1) * rows, :], x_source(m)).then_inc(s_x, 16)

            def superstep_start(n):
                m = n + 1
                if m < ITEMS:
                    sp.wait_ge(s_hcur, n + 1)
                    load_x(m)
                    sp.wait_ge(s_ids, m)
                    if m % TILES == 0:
                        load_keys(m // TILES)
                    if is_sample(m):
                        l = m // TILES
                        sp.dma_start(upper[0:HP, 0:DP], A["state_pool"][l, 0]).then_inc(s_hst, 16)
                        sp.dma_start(upper[0:HC, DP:DP + DC], A["state_dwconv"][l, 0]).then_inc(s_hst, 16)
                        sp.dma_start(upper[0:HS, DP + DC:D], A["state_shortconv"][l, 0]).then_inc(s_hst, 16)
                if n >= 2:
                    store_out(n - 2)
                if n >= 1:
                    if n >= 2:
                        sp.wait_ge(s_xost, 16 * (n - 1))
                    sp.wait_ge(s_xst, 16 * n)
                    sp.dma_start(x_out[0:width(n - 1), :], x_mid[rows_of(n - 1), :]).then_inc(s_xo, 16)

            def store_out(v):
                if v < TILES:
                    sp.wait_ge(s_yend, v + 1)
                    dst = x_mid[rows_of(v), :]
                else:
                    sp.wait_ge(s_fin, v - TILES + 1)
                    k = v % TILES
                    dst = O["y_sample"][0] if is_sample(v) else O["y_prompt"][0, k * P:(k + 1) * P, :]
                sp.dma_start(dst, x_out[0:width(v), :]).then_inc(s_xost, 16)

            def mixer_io(m):
                l = m // TILES
                if outputs_state(m):
                    o = "sample" if is_sample(m) else "prompt"
                    sp.wait_ge(s_nsc, state_count(m))
                    sp.dma_start(O["new_pool_" + o][l, 0], upper[0:HP, 0:DP]).then_inc(s_nso, 16)
                    sp.dma_start(O["new_dwconv_" + o][l, 0], upper[0:HC, DP:DP + DC]).then_inc(s_nso, 16)
                    sp.dma_start(O["new_shortconv_" + o][l, 0], upper[0:HS, DP + DC:D]).then_inc(s_nso, 16)
                more = is_sample(m) and l + 1 < DEPTH
                if more:
                    sp.wait_ge(s_proj, proj_count(m, SB))
                    load_w_in(l + 1, 0)
                    load_w_in(l + 1, 1)
                sp.wait_ge(s_x1, m + 1)
                sp.dma_start(x_mid[rows_of(m), :], x_mix[0:width(m), :]).then_inc(s_xst, 16)
                if more:
                    sp.wait_ge(s_wod, m + 1)
                    load_w(w_out, "w_out", l + 1, s_wo)
                    sp.wait_ge(s_q, 2 * (m + 1))
                    load_w(w_q, "w_q", l + 1, s_wq)

            load_x(0)
            for l in range(DEPTH):
                taps = urows[0:NCH, 0, l * DC:(l + 1) * DC]
                sp.dma_start(taps[TAP:TAP + HC + 1, :], A["w_dw"][l]).then_inc(s_prm, 16)
                sp.dma_start(taps[BIAS:BIAS + 1, :], A["b_dw"][l:l + 1, :]).then_inc(s_prm, 16)
                sp.dma_start(taps[LNG:LNG + 1, :], A["ln_g"][l:l + 1, :]).then_inc(s_prm, 16)
                sp.dma_start(taps[LNB:LNB + 1, :], A["ln_b"][l:l + 1, :]).then_inc(s_prm, 16)
                sp.dma_start(taps[STAP:NCH, :], A["w_sc"][l]).then_inc(s_prm, 16)
                for name, r, n in (("g_mix", 0, DC8), ("g_ffn", DC8, DC8), ("pool_scale", 2 * DC8, CP)):
                    sp.dma_start(urows[r:r + n, 1, l * P:(l + 1) * P],
                                 A[name][l].rearrange("(c p) -> c p", p=P)).then_inc(s_prm, 16)
            load_w_in(0, 0)
            load_w_in(0, 1)
            load_keys(0)
            load_w(w_out, "w_out", 0, s_wo)
            sp.wait_ge(s_wpz, 1)
            for l in range(DEPTH):
                for g in range(len(WINDOWS)):
                    r = 64 * (g % 2)
                    sp.dma_start(w_pool[r:r + 64, l, g // 2, r:r + 64], A["w_pool"][l, g]).then_inc(s_wp, 16)
            load_w(w_q, "w_q", 0, s_wq)
            sp.dma_start(g_fin[:, :], A["g_final"].rearrange("(a d) -> a d", a=1).partition_broadcast(P))\
                .then_inc(s_gfin, 16)
            mixer_io(0)
            for n in range(ITEMS):
                superstep_start(n)
                if n + 1 < ITEMS:
                    mixer_io(n + 1)
            superstep_start(ITEMS)
            store_out(ITEMS - 1)
            sp.wait_ge(s_xost, 16 * ITEMS)
            sp.wait_ge(s_nso, 48 * state_count(ITEMS - 1))
            sp.wait_ge(s_xst, 16 * ITEMS)

        @block.gpsimd
        def _(pool):
            nc.gpsimd.memset(ident[:, :], 0.0).then_inc(s_go, 1)
            nc.gpsimd.iota(iota_i[:, :], pattern=[[1, TOPK]], base=0, channel_multiplier=0).then_inc(s_const, 1)
            nc.gpsimd.memset(w_pool[:, :, :, :], 0.0).then_inc(s_wpz, 1)
            pool.wait_ge(s_go, 1)
            nc.gpsimd.affine_select(out=ident[:, :], in_=ident[:, :], compare_op=ALU.not_equal, fill=1.0,
                                    base=0, pattern=[[-1, P]], channel_multiplier=1).then_inc(s_const, 1)

            def fetch(rows, table, idx, item, group, j, free, staged, landed):
                pool.wait_ge(free, group * RING + (before(item) * RING + j + 1))
                nc.gpsimd.tensor_copy(idx[:, j:j + 1], ids[:, item % 3, bass.ds(group * RING + j, 1)])\
                    .then_inc(staged, 1)
                pool.wait_ge(staged, group * RING + (before(item) * RING + j + 1))
                pool.sem_inc(s_go, 1)
                nc.gpsimd.indirect_dma_start(
                    out=rows[:, j, :], out_offset=None, in_=table[:, :],
                    in_offset=bass.IndirectOffsetOnAxis(ap=idx[:, j:j + 1], axis=0)).then_inc(landed[j], 16)

            def fetch_u(n, group, j):
                fetch(urows, eu, idx_u, n, group, j, s_ufree, s_ustg, s_urow)

            def fetch_v(n, group, j):
                fetch(vrows, ev, idx_v, n - 1, group, j, s_vfree, s_vstg, s_vrow)

            for n in range(ITEMS + 1):
                if n < ITEMS:
                    pool.wait_ge(s_ids, n + 1)
                gu = groups(n) if n < ITEMS else 0
                gv = groups(n - 1) if n else 0
                with pool.Fori(0, min(g for g in (gu, gv) if g)) as t:
                    if not gu or not gv or gu == gv:
                        for j in range(RING):
                            if gu:
                                fetch_u(n, t, j)
                            if gv:
                                fetch_v(n, t, j)
                    else:
                        few, many = (fetch_u, fetch_v) if gu < gv else (fetch_v, fetch_u)
                        for i in range(RING):
                            few(n, t, i)
                            for j in range(RING):
                                many(n, t * RING + i, j)

        @block.scalar
        def _(act):
            steps = [0]

            def step(ins):
                ins.then_inc(act_step, 1)
                steps[0] += 1

            def settle():
                act.wait_ge(act_step, steps[0])

            def rms_std(src, out, rows, done):
                step(nc.scalar.activation(psA[0:rows, :], src, ACT.Square, accum_out=stat[0:rows, out:out + 1]))
                settle()
                nc.scalar.activation(stat[0:rows, out + 1:out + 2], stat[0:rows, out:out + 1], ACT.Sqrt,
                                     bias=eps[0:rows, :], scale=1.0 / D).then_inc(done, 1)

            slices = (NORM, GATE_SIGMOID, POOLING, SHORT, NORM2, FFN_H, QUERY + 1, QUERY + 3, FINISH)

            def mixer(m, tick):
                l = m // TILES
                L = width(m)
                if tick == NORM:
                    act.wait_ge(s_x, 16 * sum(loads(i) for i in range(m + 1)))
                    if m == 0:
                        act.wait_ge(s_prmS, 2)
                    else:
                        act.wait_ge(s_qT, 2 * m)
                    rms_std(x_mix[:, :], 0, P, s_std1)
                    if m % TILES == 0:
                        act.wait_ge(s_ktT, l + 1)
                        nc.scalar.copy(keysT[:, :, :], psC[:, :].rearrange("p (h n) -> p h n", h=HEADS))\
                            .then_inc(s_kT, 1)
                if tick == GATE_SIGMOID:
                    act.wait_ge(s_proj, proj_count(m, GATE))
                    act.wait_ge(s_t1, m + 1)
                    nc.scalar.activation(sig[:, :, 0:L], p_gate[:, :, 0:L], ACT.Sigmoid).then_inc(s_sig, 1)
                if tick == POOLING:
                    act.wait_ge(s_proj, proj_count(m, SH))
                    nc.scalar.copy(shc[:, :, 0:L], p_sh[:, :, 0:L]).then_inc(s_sh, 1)
                    act.wait_ge(s_d, m + 1)
                    nc.scalar.activation(sig[:, :, 0:L], zc[:, :, 0:L], ACT.Square).then_inc(s_sq, 1)
                if tick == SHORT:
                    act.wait_ge(s_var, m + 1)
                    nc.scalar.activation(lnstd[:, 0:L], psB[:, 512:512 + L], ACT.Sqrt, bias=eps[:, :],
                                         scale=1.0 / DC).then_inc(s_lstd, 1)
                    act.wait_ge(s_ya, m + 1)
                    for c in range(CP):
                        if c == 0 and m:
                            act.wait_ge(s_sc, 2 * m)
                        step(nc.scalar.activation(yT[:, c, 0:L], psC[:, c * P:c * P + L], ACT.Copy,
                                                  scale=gain[:, l, 2 * DC8 + c:2 * DC8 + c + 1]))
                    act.wait_ge(s_xhat, m + 1)
                    for c in range(CC):
                        step(nc.scalar.activation(yT[:, CP + c, 0:L], zc[:, c, 0:L], ACT.Silu,
                                                  bias=chan[:, l, c, LNB:LNB + 1], scale=chan[:, l, c, LNG:LNG + 1]))
                    settle()
                    act.sem_inc(s_yab, 1)
                if tick == NORM2:
                    act.wait_ge(s_x1, m + 1)
                    rms_std(x_mix[:, :], 2, P, s_std2)
                if tick == FFN_H:
                    act.wait_ge(s_bt, m + 1)
                    act.wait_ge(s_xst, 16 * (m + 1))
                    step(nc.scalar.copy(x_mix[:, :], psC[:, :]))
                    settle()
                    act.sem_inc(s_h, 1)
                if tick in (QUERY + 1, QUERY + 3):
                    q = (tick - QUERY) // 2
                    act.wait_ge(s_q, 2 * m + q + 1)
                    nc.scalar.copy(qT[:, 4 * q:4 * q + 4, :],
                                   psA[:, 512 * q:512 * q + 512].rearrange("p (h t) -> p h t", t=P))\
                        .then_inc(s_qT, 1)
                if tick == FINISH:
                    act.wait_ge(s_e, m + 1)
                    nc.scalar.activation(best[:, :], best[:, :], ACT.Exp).then_inc(s_exp, 1)

            def superstep_start(n):
                if n >= 1:
                    act.wait_ge(s_dots, before(n) + 1)
                    k = groups(n - 1) * RING
                    nc.scalar.activation(gelu[:, 0:k], dots[:, 0:k], ACT.Gelu).then_inc(s_gelu, 1)
                if n < ITEMS:
                    if n >= 1:
                        act.wait_ge(s_ufree, (before(n) + 1) * RING)
                    act.wait_ge(s_h, n + 1)
                    nc.scalar.copy(h_cur[:, :], x_mix[:, :]).then_inc(s_hcur, 1)

            def final_std(v):
                if v >= TILES:
                    act.wait_ge(s_yend, v + 1)
                    if v + 1 < ITEMS:
                        act.wait_ge(s_qT, 2 * min(v + 3, ITEMS))
                    rms_std(x_out[0:width(v), :], 4, width(v), s_fstd)

            def weights(item, group):
                row = group * RING + before(item) * RING
                act.wait_ge(s_diag, row + 1)
                nc.scalar.copy(coef4[:, :], coef[:, bass.ds(group * RING, RING)]).then_inc(s_coef4, 1)
                act.wait_ge(s_coef4, group + (before(item) + 1))
                for j in range(RING):
                    act.wait_ge(s_vfree, row + (j + 1))
                    nc.scalar.activation(diag[:, j, :], (fold if is_sample(item) else ident)[:, :], ACT.Copy,
                                         scale=coef4[:, j:j + 1]).then_inc(s_diag, 1)

            act.sem_inc(s_diag, 1)
            act.wait_ge(s_zero, 1)
            for tick in slices:
                mixer(0, tick)
            act.wait_ge(s_fold, 1)
            for n in range(ITEMS + 1):
                superstep_start(n)
                if n >= 2:
                    final_std(n - 2)
                if n >= 1:
                    act.wait_ge(s_coef, n)
                superstep(act, n, n - 1, slices, mixer, weights)
            final_std(ITEMS - 1)

        @block.tensor
        def _(pe):
            def turn(out, in_, rows=P):
                return nc.tensor.transpose(out, in_, ident[0:rows, 0:rows])

            def params():
                pe.wait_ge(s_const, 2)
                pe.wait_ge(s_prm, 16 * 8 * DEPTH)
                for l in range(DEPTH):
                    for c in range(CC):
                        o = (l * CC + c) * 64
                        turn(psB[:, o:o + NCH], urows[0:NCH, 0, l * DC + c * P:l * DC + (c + 1) * P], NCH)
                for l in range(DEPTH):
                    n = 2 * DC8 + CP
                    last = turn(psC[:, l * 64:l * 64 + n], urows[0:n, 1, l * P:(l + 1) * P], n)
                last.then_inc(s_prmT, 1)

            def queries(q):
                for h in range(2 * q, 2 * q + 2):
                    for c in range(DC8):
                        last = nc.tensor.matmul(psA[:, h * P:(h + 1) * P], w_q[:, c, h * P:(h + 1) * P],
                                                hT[:, c, :], start=c == 0, stop=c == DC8 - 1)
                if q % 2:
                    last.then_inc(s_q, 1)

            def scores(m, q):
                pe.wait_ge(s_qT, 2 * m + q + 1)
                dst = psC if q else psB
                for h in range(4):
                    for half in range(2):
                        r = slice(half * DH, (half + 1) * DH)
                        o = 512 * half + NK * h
                        last = nc.tensor.matmul(dst[:, o:o + NK], qT[r, 4 * q + h, :], keysT[r, 4 * q + h, :],
                                                start=True, stop=True)
                last.then_inc(s_sc, 1)

            slices = (NORM, *PROJ_TICKS, POOLING, SHORT, *range(W_OUT, W_OUT + W_OUT_TICKS), NORM2,
                      *range(QUERY, QUERY + QUERY_TICKS))

            def mixer(m, tick):
                l = m // TILES
                L = width(m)
                if tick == NORM:
                    if m % TILES == 0:
                        pe.wait_ge(s_kst, 16 * (l + 1))
                        if m:
                            pe.wait_ge(s_ids, m)
                        else:
                            pe.wait_ge(s_prmS, 2)
                        for h in range(HEADS):
                            last = turn(psC[:, h * P:(h + 1) * P], upper[:, h * P:(h + 1) * P])
                        last.then_inc(s_ktT, 1)
                    if is_sample(m):
                        pe.wait_ge(s_hst, 48 * (l + 1))
                        pe.wait_ge(s_ids, m)
                        for i, (_, _, rows) in enumerate(STATE_CHUNKS):
                            last = turn(psC[:, i * 32:i * 32 + rows], upper[0:rows, i * P:(i + 1) * P], rows)
                        last.then_inc(s_hstT, 1)
                    pe.wait_ge(s_xn, m + 1)
                    for c in range(DC8):
                        last = turn(psA[:, c * P:(c + 1) * P], xn[:, c * P:(c + 1) * P])
                    last.then_inc(s_t1, 1)
                if tick in proj_of:
                    first = list(proj_of).index(tick)
                    if first == 0:
                        pe.wait_ge(s_hT, m + 1)
                        pe.wait_ge(s_wi[0], 16 * (l + 1))
                        if m:
                            pe.wait_ge(s_ids, m)
                    if last_chunk[first] > VAL and last_chunk[first - 1] <= VAL:
                        if is_sample(m):
                            pe.wait_ge(s_hist, l + 1)
                        pe.wait_ge(s_kT, l + 1)
                    if last_chunk[first] > U and last_chunk[first - 1] <= U:
                        pe.wait_ge(s_wi[1], 16 * (l + 1))
                    for col, dst, c in proj_of[tick]:
                        for k in range(DC8):
                            last = nc.tensor.matmul(dst[:, c, 0:L], w_in[:, k, col:col + P], hT[:, k, 0:L],
                                                    start=k == 0, stop=k == DC8 - 1)
                    last.then_inc(s_proj, 1)
                if tick == POOLING:
                    pe.wait_ge(s_zc, m + 1)
                    for c in range(CC):
                        last = nc.tensor.matmul(psB[:, 0:L], ones[:, :], zc[:, c, 0:L],
                                                start=c == 0, stop=c == CC - 1)
                    last.then_inc(s_mean, 1)
                    pe.wait_ge(s_sq, m + 1)
                    for c in range(CC):
                        last = nc.tensor.matmul(psB[:, 512:512 + L], ones[:, :], sig[:, c, 0:L],
                                                start=c == 0, stop=c == CC - 1)
                    last.then_inc(s_var, 1)
                if tick == SHORT:
                    pe.wait_ge(s_wp, 16 * DEPTH * len(WINDOWS))
                    pe.wait_ge(s_pd, m + 1)
                    for c in range(CP):
                        last = nc.tensor.matmul(psC[:, c * P:c * P + L], w_pool[:, l, c, :], pdif[:, c, 0:L],
                                                start=True, stop=True)
                    last.then_inc(s_ya, 1)
                if tick == W_OUT:
                    pe.wait_ge(s_yab, m + 1)
                    pe.wait_ge(s_yc, m + 1)
                    if outputs_state(m):
                        for i, (buf, c, rows) in enumerate(STATE_CHUNKS):
                            last = turn(psC[0:rows, i * P:(i + 1) * P], buf[:, c, L:L + rows])
                        last.then_inc(s_nst, 1)
                    pe.wait_ge(s_wo, 16 * (l + 1))
                if W_OUT <= tick < W_OUT + W_OUT_TICKS:
                    o, c0 = 512 * ((tick - W_OUT) // 2), DC8 // 2 * ((tick - W_OUT) % 2)
                    for c in range(c0, c0 + DC8 // 2):
                        last = nc.tensor.matmul(psA[:, o:o + 512], yT[:, c, :], w_out[:, c, o:o + 512],
                                                start=c == 0, stop=c == DC8 - 1)
                    if tick == W_OUT + W_OUT_TICKS - 1:
                        last.then_inc(s_wod, 1)
                if tick == NORM2:
                    pe.wait_ge(s_xn2, m + 1)
                    for c in range(DC8):
                        last = turn(psB[:, c * P:(c + 1) * P], xn[:, c * P:(c + 1) * P])
                    last.then_inc(s_t2, 1)
                if tick == FFN_H:
                    pe.wait_ge(s_hT2, m + 1)
                    if outputs_state(m):
                        pe.wait_ge(s_nsc, state_count(m))
                    for c in range(DC8):
                        last = turn(psC[:, c * P:(c + 1) * P], hT[:, c, :])
                    last.then_inc(s_bt, 1)
                    pe.wait_ge(s_wq, 16 * (l + 1))
                if QUERY <= tick < QUERY + QUERY_TICKS:
                    pair = tick - QUERY
                    queries(pair)
                    if pair == 3:
                        pe.wait_ge(s_h, m + 1)
                    if pair % 2:
                        scores(m, pair // 2)

            def clear(start):
                for half in (0, 512):
                    last = nc.tensor.matmul(yacc[:, half:half + 512], zeros[:, 0:P], zeros[:, :],
                                            start=start, stop=not start, skip_group_check=True)
                return last

            def add_rows(item, group):
                row = group * RING + before(item) * RING
                for j in range(RING):
                    pe.wait_ge(s_vrow[j], group * 16 + (before(item) * 16 + 16))
                    pe.wait_ge(s_diag, row + (j + 2))
                    for half in (0, 512):
                        last = nc.tensor.matmul(yacc[:, half:half + 512], diag[:, j, :],
                                                vrows[:, j, half:half + 512], start=False, stop=False,
                                                skip_group_check=True)
                    last.then_inc(s_vfree, 1)

            pe.sem_inc(s_vfree, RING)
            params()
            for tick in slices:
                mixer(0, tick)
            pe.wait_ge(s_zero, 1)
            for n in range(ITEMS + 1):
                if n >= 1:
                    if n >= 2:
                        pe.wait_ge(s_yend, n - 1)
                    clear(True)
                superstep(pe, n, n - 1, slices, mixer, add_rows)
                if n >= 1:
                    clear(False).then_inc(s_ysum, 1)

        @block.vector
        def _(dve):
            steps = [0]

            def step(ins):
                ins.then_inc(dve_step, 1)
                steps[0] += 1

            def settle(back=0):
                if steps[0] > back:
                    dve.wait_ge(dve_step, steps[0] - back)

            def chain(ins):
                step(ins)
                settle()

            def consts():
                nc.vector.memset(eps[:, :], EPS)
                nc.vector.memset(ones[:, :], 1.0)
                nc.vector.memset(zeros[:, :], 0.0)
                chain(nc.vector.memset(stat[:, :], 0.0))
                dve.sem_inc(s_zero, 1)
                dve.wait_ge(s_const, 2)
                for q in range(COPIES):
                    r = slice(q * LS, (q + 1) * LS)
                    step(nc.vector.tensor_copy(
                        fold[r, :].rearrange("p (q t) -> p q t", q=COPIES),
                        ident[r, r].unsqueeze(1).to_broadcast([LS, COPIES, LS])))
                chain(nc.vector.tensor_copy(iota_f[:, :], iota_i[:, :]))
                dve.sem_inc(s_fold, 1)
                for g, w in enumerate(WINDOWS):
                    r = slice(64 * (g % 2), 64 * (g % 2) + 64)
                    step(nc.vector.tensor_scalar(rcnt[r, g // 2, :], iota_f[r, :], 1.0, float(w), ALU.add, ALU.min))
                settle()
                chain(nc.vector.reciprocal(rcnt[:, :, :], rcnt[:, :, :]))
                dve.wait_ge(s_prmT, 1)
                nc.vector.tensor_copy(
                    chan[:, :, :, :].rearrange("p l c r -> p (l c) r"),
                    psB[:, 0:DEPTH * CC * 64].rearrange("p (g r) -> p g r", r=64)[:, :, 0:NCH]).then_inc(s_prmS, 1)
                nc.vector.tensor_copy(
                    gain[:, :, :],
                    psC[:, 0:DEPTH * 64].rearrange("p (g r) -> p g r", r=64)[:, :, 0:2 * DC8 + CP])\
                    .then_inc(s_prmS, 1)
                dve.wait_ge(s_prmS, 2)

            def norm(src, col, out, rows=P):
                chain(nc.vector.reciprocal(stat[0:rows, col + 1:col + 2], stat[0:rows, col + 1:col + 2]))
                return nc.vector.tensor_scalar(out, src, stat[0:rows, col + 1:col + 2], None, ALU.mult)

            def scale_turned(ps_src, l, first):
                return nc.vector.tensor_tensor(
                    hT[:, :, :], ps_src[:, :].rearrange("p (c t) -> p c t", t=P),
                    gain[:, l, first:first + DC8].unsqueeze(2).to_broadcast([P, DC8, P]), ALU.mult)

            def taps(m, lo, hi):
                l, L = m // TILES, width(m)
                for k in range(lo, hi):
                    for c in range(CC):
                        z = zbuf[:, c, k:k + L]
                        w = chan[:, l, c, k:k + 1]
                        settle(CC - 1 if k else 0)
                        if k == 0:
                            step(nc.vector.tensor_scalar(zc[:, c, 0:L], z, w, chan[:, l, c, BIAS:BIAS + 1],
                                                         ALU.mult, ALU.add))
                        else:
                            step(nc.vector.scalar_tensor_tensor(out=zc[:, c, 0:L], in0=z, scalar=w,
                                                                in1=zc[:, c, 0:L], op0=ALU.mult, op1=ALU.add))

            def histories(m, which):
                for i, (buf, h) in enumerate(((ubuf, HP), (zbuf, HC), (mbuf, HS))):
                    if i not in which:
                        continue
                    if m % TILES == 0:
                        chain(nc.vector.memset(buf[:, :, 0:h], 0.0))
                    elif not is_sample(m):
                        chain(nc.vector.tensor_copy(buf[:, :, 0:h], buf[:, :, P:P + h]))

            def pool_windows(m):
                L = width(m)
                E = HP + L
                dve.wait_ge(s_proj, proj_count(m, U))
                chain(nc.vector.tensor_copy(ubuf[:, :, HP:E], p_u[:, :, 0:L]))
                chain(nc.vector.tensor_tensor(win_a[:, :, 1:E], ubuf[:, :, 1:E], ubuf[:, :, 0:E - 1], ALU.add))
                chain(nc.vector.tensor_tensor(win_b[:, :, 3:E], win_a[:, :, 3:E], win_a[:, :, 1:E - 2], ALU.add))
                chain(nc.vector.tensor_tensor(win_a[:, 1, 7:E], win_b[:, 1, 7:E], win_b[:, 1, 3:E - 4], ALU.add))
                chain(nc.vector.tensor_tensor(win_b[64:128, 1, 15:E], win_a[64:128, 1, 15:E],
                                              win_a[64:128, 1, 7:E - 8], ALU.add))
                sums = (win_a, win_b, win_a, win_b)
                for g, w in enumerate(WINDOWS):
                    r, c = slice(64 * (g % 2), 64 * (g % 2) + 64), g // 2
                    step(nc.vector.scalar_tensor_tensor(
                        out=pdif[r, c, 0:L], in0=sums[g][r, c, HP:E], scalar=1.0 / w,
                        in1=ubuf[r, c, HP:E], op0=ALU.mult, op1=ALU.subtract))
                settle()
                if m % TILES == 0:
                    for g in range(len(WINDOWS)):
                        r, c = slice(64 * (g % 2), 64 * (g % 2) + 64), g // 2
                        step(nc.vector.tensor_tensor(pdif[r, c, 0:TOPK], sums[g][r, c, HP:HP + TOPK],
                                                     rcnt[r, c, :], ALU.mult))
                    settle()
                    chain(nc.vector.tensor_tensor(pdif[:, :, 0:TOPK], pdif[:, :, 0:TOPK],
                                                  ubuf[:, :, HP:HP + TOPK], ALU.subtract))
                dve.sem_inc(s_pd, 1)

            def short_conv(m):
                l, L = m // TILES, width(m)
                dve.wait_ge(s_sh, m + 1)
                dve.wait_ge(s_proj, proj_count(m, SB))
                if m:
                    dve.wait_ge(s_sc, 2 * m)
                chain(nc.vector.tensor_tensor(mbuf[:, :, HS:HS + L], p_sc[:, :, 0:L], shc[:, :, 0:L], ALU.mult))
                for k in range(HS + 1):
                    for c in range(CS):
                        x, w = mbuf[:, c, k:k + L], chan[:, l, c, STAP + k:STAP + k + 1]
                        settle(CS - 1 if k else 0)
                        if k == 0:
                            step(nc.vector.tensor_scalar(shc[:, c, 0:L], x, w, None, ALU.mult))
                        else:
                            step(nc.vector.scalar_tensor_tensor(out=shc[:, c, 0:L], in0=x, scalar=w,
                                                                in1=shc[:, c, 0:L], op0=ALU.mult, op1=ALU.add))
                settle()
                step(nc.vector.tensor_tensor(yT[:, CP + CC:DC8, 0:L], p_sb[:, :, 0:L], shc[:, :, 0:L], ALU.mult))
                settle()
                if not is_sample(m):
                    dve.sem_inc(s_yc, 1)

            def top16(values, scratch, out_v, out_i):
                chain(nc.vector.max(out_v[:, 0:8], values))
                step(nc.vector.max_index(out_i[:, 0:8], out_v[:, 0:8], values))
                chain(nc.vector.match_replace(scratch, out_v[:, 0:8], values, LOWEST))
                chain(nc.vector.max(out_v[:, 8:16], scratch))
                chain(nc.vector.max_index(out_i[:, 8:16], out_v[:, 8:16], scratch))

            def top_keys(m, pair):
                q = pair // 2
                src = psC if q else psB
                dve.wait_ge(s_sc, 2 * m + q + 1)
                if pair == 0 and outputs_state(m):
                    dve.wait_ge(s_nso, 48 * state_count(m))
                for h in range(2):
                    for half in range(2):
                        o = 512 * half + NK * (2 * (pair % 2) + h)
                        top16(src[:, o:o + NK], wk128, tv[:, h, half, :], ti[:, h, half, :])
                chain(nc.vector.tensor_copy(tif[:, :, :, :], ti[:, :, :, :]))

            def top_sums(m, pair):
                for h in range(2):
                    step(nc.vector.tensor_tensor(
                        cand[:, h, :, :], tv[:, h, 0, :].unsqueeze(2).to_broadcast([P, TOPK, TOPK]),
                        tv[:, h, 1, :].unsqueeze(1).to_broadcast([P, TOPK, TOPK]), ALU.add))
                settle()
                for h in range(2):
                    b = best[:, (2 * pair + h) * TOPK:(2 * pair + h + 1) * TOPK]
                    top16(cand[:, h, :, :].rearrange("p a b -> p (a b)"), wk256, b, bj[:, h, :])

            def experts(m, pair):
                step(nc.vector.tensor_scalar(ab[:, 0, :, :], bj[:, :, :], 4, None, ALU.logical_shift_right))
                step(nc.vector.tensor_scalar(ab[:, 1, :, :], bj[:, :, :], TOPK - 1, None, ALU.bitwise_and))
                settle()
                chain(nc.vector.tensor_copy(abf[:, :, :, :], ab[:, :, :, :]))
                for half in range(2):
                    chain(nc.vector.tensor_tensor(
                        onehot[:, :, :, :], abf[:, half, :, :].unsqueeze(3).to_broadcast([P, 2, TOPK, TOPK]),
                        iota_f[:, :].unsqueeze(1).unsqueeze(1).to_broadcast([P, 2, TOPK, TOPK]), ALU.is_equal))
                    chain(nc.vector.tensor_tensor(
                        onehot[:, :, :, :], onehot[:, :, :, :],
                        tif[:, :, half, :].unsqueeze(2).to_broadcast([P, 2, TOPK, TOPK]), ALU.mult))
                    chain(nc.vector.tensor_reduce(ij[:, half, :, :], onehot[:, :, :, :], AX.X, ALU.add))
                o = 2 * pair * TOPK
                chain(nc.vector.scalar_tensor_tensor(
                    out=idf[:, o:o + 2 * TOPK], in0=ij[:, 0, :, :].rearrange("p h k -> p (h k)"),
                    scalar=float(NK), in1=ij[:, 1, :, :].rearrange("p h k -> p (h k)"),
                    op0=ALU.mult, op1=ALU.add))

            def finish_routing(m):
                b3 = best[:, :].rearrange("p (h k) -> p h k", k=TOPK)
                chain(nc.vector.tensor_copy(hsum[:, :], b3[:, :, 0]))
                chain(nc.vector.tensor_tensor(b3, b3, hsum[:, :].unsqueeze(2).to_broadcast([P, HEADS, TOPK]),
                                              ALU.subtract))
                dve.sem_inc(s_e, 1)
                base = float(m // TILES * NE)
                spans = [(slice(q * LS, (q + 1) * LS), slice(q * 32, q * 32 + 32)) for q in range(COPIES)] \
                    if is_sample(m) else [(slice(0, P), slice(0, KPICK))]
                for r, cols in spans:
                    n = cols.stop - cols.start
                    step(nc.vector.tensor_scalar(ids[r, m % 3, 0:n], idf[r, cols], base, None, ALU.add))
                dve.wait_ge(s_exp, m + 1)
                chain(nc.vector.tensor_reduce(hsum[:, :], b3, AX.X, ALU.add))
                chain(nc.vector.reciprocal(hsum[:, :], hsum[:, :]))
                chain(nc.vector.tensor_tensor(b3, b3, hsum[:, :].unsqueeze(2).to_broadcast([P, HEADS, TOPK]),
                                              ALU.mult))
                for r, cols in spans:
                    n = cols.stop - cols.start
                    step(nc.vector.tensor_copy(gates[r, m % 2, 0:n], best[r, cols]))
                settle()
                dve.sem_inc(s_ids, 1)

            TAPS = HC // CONV_TICKS + 1
            slices = (NORM, *range(CONV, CONV + CONV_TICKS), POOLING, SHORT, W_OUT, W_OUT + 2, NORM2, FFN_H,
                      *range(ROUTE, ROUTE + 3 * HEADS // 2), FINISH)

            def mixer(m, tick):
                l, L = m // TILES, width(m)
                if tick == NORM:
                    dve.wait_ge(s_std1, m + 1)
                    norm(x_mix[:, :], 0, xn).then_inc(s_xn, 1)
                    if is_sample(m):
                        dve.wait_ge(s_hstT, l + 1)
                        ph = psC[:, 0:256].rearrange("p (i t) -> p i t", t=32)
                        step(nc.vector.tensor_copy(ubuf[:, :, 0:HP], ph[:, 0:CP, 0:HP]))
                        step(nc.vector.tensor_copy(zbuf[:, :, 0:HC], ph[:, CP:CP + CC, 0:HC]))
                        step(nc.vector.tensor_copy(mbuf[:, :, 0:HS], ph[:, CP + CC:DC8, 0:HS]))
                        settle()
                        dve.sem_inc(s_hist, 1)
                    dve.wait_ge(s_t1, m + 1)
                    scale_turned(psA, l, 0).then_inc(s_hT, 1)
                if tick == CONV:
                    histories(m, (1,))
                    dve.wait_ge(s_sig, m + 1)
                    dve.wait_ge(s_proj, proj_count(m, VAL))
                    chain(nc.vector.tensor_tensor(zbuf[:, :, HC:HC + L], p_val[:, :, 0:L], sig[:, :, 0:L], ALU.mult))
                if CONV <= tick < CONV + CONV_TICKS:
                    taps(m, TAPS * (tick - CONV), min(TAPS * (tick - CONV + 1), HC + 1))
                if tick == CONV + CONV_TICKS - 1:
                    settle()
                    dve.sem_inc(s_zc, 1)
                if tick == POOLING:
                    dve.wait_ge(s_mean, m + 1)
                    nc.vector.scalar_tensor_tensor(
                        out=zc[:, :, 0:L], in0=psB[:, 0:L].unsqueeze(1).to_broadcast([P, CC, L]),
                        scalar=-1.0 / DC, in1=zc[:, :, 0:L], op0=ALU.mult, op1=ALU.add).then_inc(s_d, 1)
                    histories(m, (0, 2))
                    pool_windows(m)
                if tick == SHORT:
                    dve.wait_ge(s_lstd, m + 1)
                    chain(nc.vector.reciprocal(lnstd[:, 0:L], lnstd[:, 0:L]))
                    nc.vector.tensor_tensor(zc[:, :, 0:L], zc[:, :, 0:L],
                                            lnstd[:, 0:L].unsqueeze(1).to_broadcast([P, CC, L]), ALU.mult)\
                        .then_inc(s_xhat, 1)
                    short_conv(m)
                if tick == W_OUT and is_sample(m):
                    dve.wait_ge(s_yab, m + 1)
                    chain(nc.vector.tensor_copy(
                        yT[:, :, L:P].rearrange("p c (q t) -> p c q t", t=L),
                        yT[:, :, 0:L].unsqueeze(2).to_broadcast([P, DC8, COPIES - 1, L])))
                    dve.sem_inc(s_yc, 1)
                if tick == W_OUT + 2 and outputs_state(m):
                    dve.wait_ge(s_nst, state_count(m))
                    for rows, cols in ((HP, slice(0, DP)), (HC, slice(DP, DP + DC)), (HS, slice(DP + DC, D))):
                        step(nc.vector.tensor_copy(upper[0:rows, cols], psC[0:rows, cols]))
                    settle()
                    dve.sem_inc(s_nsc, 1)
                if tick == NORM2:
                    dve.wait_ge(s_wod, m + 1)
                    nc.vector.tensor_tensor(x_mix[:, :], psA[:, :], x_mix[:, :], ALU.add).then_inc(s_x1, 1)
                    dve.wait_ge(s_std2, m + 1)
                    norm(x_mix[:, :], 2, xn).then_inc(s_xn2, 1)
                if tick == FFN_H:
                    dve.wait_ge(s_t2, m + 1)
                    scale_turned(psB, l, DC8).then_inc(s_hT2, 1)
                if ROUTE <= tick < FINISH:
                    pair, stage = divmod(tick - ROUTE, 3)
                    (top_keys, top_sums, experts)[stage](m, pair)
                if tick == FINISH:
                    finish_routing(m)

            def take_sums(v):
                rows = width(v)
                dve.wait_ge(s_ysum, v + 1)
                dve.wait_ge(s_xo, 16 * (v + 1))
                nc.vector.tensor_tensor(x_out[0:rows, :], yacc[0:rows, :], x_out[0:rows, :], ALU.add)\
                    .then_inc(s_yend, 1)

            def final_norm(v):
                rows = width(v)
                dve.wait_ge(s_gfin, 16)
                dve.wait_ge(s_fstd, v - TILES + 1)
                chain(norm(x_out[0:rows, :], 4, x_out[0:rows, :], rows))
                nc.vector.tensor_tensor(x_out[0:rows, :], x_out[0:rows, :], g_fin[0:rows, :], ALU.mult)\
                    .then_inc(s_fin, 1)

            def dot_rows(item, group):
                row = group * RING + before(item) * RING
                dve.wait_ge(s_dots, group + (before(item) + 1))
                for j in range(RING):
                    dve.wait_ge(s_urow[j], group * 16 + (before(item) * 16 + 16))
                    nc.vector.tensor_tensor_reduce(urows[:, j, :], urows[:, j, :], h_cur[:, :], 1.0, 0.0,
                                                   ALU.mult, ALU.add, dots4[:, j:j + 1]).then_inc(s_ufree, 1)
                dve.wait_ge(s_ufree, row + 2 * RING)
                nc.vector.tensor_copy(dots[:, bass.ds(group * RING, RING)], dots4[:, :]).then_inc(s_dots, 1)

            dve.sem_inc(s_ufree, RING)
            dve.sem_inc(s_dots, 1)
            consts()
            for tick in slices:
                mixer(0, tick)
            for n in range(ITEMS + 1):
                if n >= 2:
                    take_sums(n - 2)
                if n >= 1:
                    k = groups(n - 1) * RING
                    dve.wait_ge(s_gelu, n)
                    nc.vector.tensor_tensor(coef[:, 0:k], gelu[:, 0:k], gates[:, (n - 1) % 2, 0:k], ALU.mult)\
                        .then_inc(s_coef, 1)
                if n - 2 >= TILES:
                    final_norm(n - 2)
                if n < ITEMS:
                    dve.wait_ge(s_hcur, n + 1)
                superstep(dve, n, n, slices, mixer, dot_rows)
            take_sums(ITEMS - 1)
            final_norm(ITEMS - 1)


_INS = ['x_prompt', 'x_sample', 'state_pool', 'state_dwconv', 'state_shortconv', 'g_mix', 'w_in', 'w_pool',
        'pool_scale', 'w_dw', 'b_dw', 'ln_g', 'ln_b', 'w_sc', 'w_out', 'g_ffn', 'w_q', 'sub_keys', 'expert_u',
        'expert_v', 'g_final']
_OUTS = ['y_prompt', 'y_sample', 'new_pool_prompt', 'new_dwconv_prompt', 'new_shortconv_prompt',
         'new_pool_sample', 'new_dwconv_sample', 'new_shortconv_sample']


def kernel(**inputs):
    import numpy as _np
    import concourse.bacc as _bacc
    from concourse import mybir as _mybir
    from concourse.bass_utils import run_bass_kernel_spmd as _run

    nc = _bacc.Bacc("TRN2", target_bir_lowering=False, num_devices=1, dynamic_dma_scratch_size=4096)
    arrays, ins, outs = {}, {}, {}
    for name in _INS:
        a = _np.ascontiguousarray(inputs[name])
        arrays[f"in_{name}"] = a
        ins[name] = nc.dram_tensor(f"in_{name}", a.shape, _mybir.dt.from_np(a.dtype), kind="ExternalInput").ap()
    shape = {n: inputs[n].shape for n in _INS}
    batch = shape['x_prompt'][0]
    out_shapes = [shape['x_prompt'], shape['x_sample']]
    for _ in range(2):
        out_shapes += [(s[0], batch) + tuple(s[2:]) for s in
                       (shape['state_pool'], shape['state_dwconv'], shape['state_shortconv'])]
    for name, s in zip(_OUTS, out_shapes):
        outs[name] = nc.dram_tensor(f"out_{name}", tuple(s), _mybir.dt.float32, kind="ExternalOutput").ap()
    build(nc, ins, outs)
    r = _run(nc, [arrays], core_ids=[0])
    return tuple(r.results[0][f"out_{name}"] for name in _OUTS)
```

```python
from contextlib import ExitStack

import concourse.bass as bass
from concourse import mybir

ALU = mybir.AluOpType
ACT = mybir.ActivationFunctionType
AX = mybir.AxisListType
F32 = mybir.dt.float32
BF16 = mybir.dt.bfloat16
U32 = mybir.dt.uint32
I32 = mybir.dt.int32

P = 128
RING = 4
TICKS = 32
EPS = 1e-6
LOWEST = -3.0e38


NORM, GATE_SIGMOID, CONV, POOLING, SH_COPY, SHORT, CENTRE, SCALE, W_OUT, NORM2, FFN_H, QUERY, ROUTE, FINISH = \
    1, 4, 5, 7, 8, 9, 9, 10, 11, 15, 16, 16, 18, 30
PROJ_TICKS = {2: 3, 3: 3, 4: 2, 5: 2, 6: 3, 7: 2, 8: 2}
QUERY_TICKS = CONV_TICKS = 4

EVEN = [(0, TICKS, 0, 0, 32)]
U_PLAN = [
    EVEN, EVEN, EVEN,
    [(0, 16, 0, 0, 16), (16, 28, 0, 16, 22)],
    [(0, 10, 1, 22, 32), (10, 18, 0, 0, 8)],
    EVEN, EVEN, EVEN, EVEN,
    [(0, TICKS, 0, 0, 8)],
    [],
]
LATER = [(0, 16, 1, 14, 30), (16, 18, 1, 30, 32), (18, 32, 0, 0, 14)]
V_PLAN = [
    [(6, 16, 0, 0, 10), (20, 32, 0, 10, 22)],
    [(0, 10, 1, 22, 32), (18, 32, 0, 0, 14)],
    [(0, 10, 1, 14, 24), (18, 26, 1, 24, 32), (26, 32, 0, 0, 6)],
    [(0, 10, 1, 6, 16), (16, 32, 1, 16, 32)],
    [(0, 10, 1, 0, 10), (18, 32, 1, 10, 24)],
    [(0, 8, 2, 24, 32), (8, 16, 1, 0, 8), (18, 32, 0, 0, 14)],
    LATER, LATER, LATER,
    [(0, 16, 1, 14, 30), (16, 18, 1, 30, 32), (18, 32, 0, 0, 4)],
    [(0, 4, 1, 4, 8)],
]
WEIGH = [(4, 8, 12, 18, 24), (0, 16,), (0, 24,), (0,), (0, 10), (0, 16,), (0, 16,), (0, 16,), (0, 16,), (0, 16,), (0,)]
WEIGH_LAG = 2
FINAL_STD, FINAL_NORM = 20, 22


def build(nc, A, O):
    DEPTH, D = A["g_mix"].shape
    SEQ, LS = A["x_prompt"].shape[1], A["x_sample"].shape[1]
    DP, DC, DSC = A["state_pool"].shape[3], A["state_dwconv"].shape[3], A["state_shortconv"].shape[3]
    HP, HC, HS = A["state_pool"].shape[2], A["state_dwconv"].shape[2], A["state_shortconv"].shape[2]
    NE = A["expert_u"].shape[1]
    HEADS, NK, DH = A["sub_keys"].shape[1], A["sub_keys"].shape[3], A["sub_keys"].shape[4]
    TOPK = 16
    KPICK = HEADS * TOPK
    DC8 = D // P
    CP, CC, CS = DP // P, DC // P, DSC // P
    D_IN = DP + 2 * DC + 3 * DSC
    WINDOWS = (2, 4, 8, 16)
    TILES = SEQ // P + 1
    ITEMS = DEPTH * TILES
    COPIES = P // LS
    assert (CP, CC, CS, DC8, KPICK, NK, DH, COPIES) == (2, 3, 3, 8, 128, 128, 64, 4)

    def is_sample(m):
        return m % TILES == TILES - 1

    def width(m):
        return LS if is_sample(m) else P

    def loads(m):
        return COPIES if is_sample(m) else 1

    def groups(m):
        return (KPICK // COPIES if is_sample(m) else KPICK) // RING

    def before(m):
        return sum(groups(i) for i in range(m))

    def spans_of(plan, n):
        return [(t0, t1, n - back, g0, g1) for t0, t1, back, g0, g1 in plan[n]]

    def u_spans(n):
        return spans_of(U_PLAN, n)

    def v_spans(n):
        return spans_of(V_PLAN, n)

    def part(span, tick, upto):
        t0, t1, _, g0, g1 = span
        return [g0 + (min(max(t, t0), t1) - t0) * (g1 - g0) // (t1 - t0) for t in (tick, upto)]

    def v_starts(n):
        return [(t0, v) for t0, _, v, g0, _ in v_spans(n) if g0 == 0]

    def v_ends(n):
        return [(t1, v) for _, t1, v, _, g1 in v_spans(n) if g1 == groups(v)]

    def dots_done(v, n, tick):
        return max([0] + [part(s, 0, tick if k == n else TICKS)[1] for k in range(n + 1) for s in u_spans(k)
                          if s[2] == v and (k < n or s[0] < tick)])

    WEIGHINGS, weighed_to = [], [0] * ITEMS
    for n in range(ITEMS + 1):
        for tick in WEIGH[n]:
            for v in range(ITEMS):
                done = dots_done(v, n, tick)
                if done > weighed_to[v]:
                    WEIGHINGS.append((n, tick, v, weighed_to[v], done))
                    weighed_to[v] = done

    def weighings(n):
        return [(tick, count, v, g0, g1) for count, (k, tick, v, g0, g1) in enumerate(WEIGHINGS) if k == n]

    everything = [(v, g) for v in range(ITEMS) for g in range(groups(v))]
    for plan in (U_PLAN, V_PLAN):
        assert len(plan) == len(WEIGH) == ITEMS + 1 and everything == \
            [(v, g) for n in range(ITEMS + 1) for _, _, v, g0, g1 in spans_of(plan, n) for g in range(g0, g1)]
    for n in range(ITEMS + 1):
        for t0, t1, v, g0, g1 in v_spans(n):
            for i in range(g1 - g0):
                assert any(w == v and g0 + i < end and
                           (k, tick + WEIGH_LAG if tick else 0) <= (n, t0 + i * (t1 - t0) // (g1 - g0))
                           for k, tick, w, _, end in WEIGHINGS)

    def outputs_state(m):
        return m % TILES >= TILES - 2

    def state_count(m):
        return sum(outputs_state(i) for i in range(m + 1))

    eu = A["expert_u"].rearrange("l e d -> (l e) d")
    ev = A["expert_v"].rearrange("l e d -> (l e) d")

    with ExitStack() as ctx:
        def sb(name, shape, dt=F32):
            return ctx.enter_context(nc.sbuf_tensor(name, shape, dt))

        def ps(name):
            return ctx.enter_context(nc.psum_tensor(name, [P, 1024], F32))

        def sem(name):
            return ctx.enter_context(nc.semaphore(name))

        w_in = sb("w_in_sb", [P, DC8, D_IN])
        w_out = sb("w_out_sb", [P, DC8, D])
        w_q = sb("w_q_sb", [P, DC8, D])
        keysT = sb("keysT", [P, HEADS, NK])
        urows = sb("urows", [P, RING, D])
        vrows = sb("vrows", [P, RING, D])
        diag = sb("diag", [P, RING, P])
        h_cur = sb("h_cur", [P, D])
        x_mix = sb("x_mix", [P, D])
        x_out = sb("x_out", [P, D])
        g_fin = sb("g_fin", [P, D])
        hT = sb("hT", [P, DC8, P])
        yT = sb("yT", [P, DC8, P])
        qT = yT
        work = sb("work", [P, 2048])
        zbuf = sb("zbuf", [P, CC, HC + P])
        ubuf = sb("ubuf", [P, CP, HP + P])
        mbuf = sb("mbuf", [P, CS, HS + P])
        ids = sb("ids", [P, 3, KPICK], U32)
        gates = sb("gates", [P, 2, KPICK])
        dots = sb("dots", [P, KPICK])
        dots4 = sb("dots4", [P, RING])
        gelu = sb("gelu", [P, KPICK])
        coef = sb("coef", [P, KPICK])
        coef4 = sb("coef4", [P, RING])
        idf = sb("idf", [P, KPICK])
        best = sb("best", [P, KPICK])
        ident = sb("ident", [P, P])
        fold = sb("fold", [P, P])
        ones = sb("ones", [P, P])
        zeros = sb("zeros", [P, 512], BF16)
        w_pool = sb("w_pool_sb", [P, DEPTH, CP, P])
        chan = sb("chan", [P, DEPTH, CC, HC + 1 + 3 + HS + 1])
        gain = sb("gain", [P, DEPTH, 2 * DC8 + CP])
        stat = sb("stat", [P, 8])
        hsum = sb("hsum", [P, HEADS])
        iota_i = sb("iota_i", [P, TOPK], I32)
        iota_f = sb("iota_f", [P, TOPK])
        rcnt = sb("rcnt", [P, CP, TOPK])
        idx_u = sb("idx_u", [P, 2 * RING], U32)
        idx_v = sb("idx_v", [P, 2 * RING], U32)
        eps = sb("eps", [P, 1])
        x_mid = nc.dram_tensor("x_mid", [SEQ + LS, D], F32).ap()

        NCH = HC + 1 + 3 + HS + 1
        TAP, BIAS, LNG, LNB, STAP = 0, HC + 1, HC + 2, HC + 3, HC + 4

        xn = work[:, 0:1024]
        upper = work[:, 1024:2048]
        zc = work[:, 0:384].rearrange("p (c t) -> p c t", c=CC)
        sig = work[:, 384:768].rearrange("p (c t) -> p c t", c=CC)
        lnstd = work[:, 384:512]
        win_a = work[:, 768:768 + CP * (HP + P)].rearrange("p (c t) -> p c t", c=CP)
        win_b = work[:, 1056:1056 + CP * (HP + P)].rearrange("p (c t) -> p c t", c=CP)
        pdif = work[:, 1344:1600].rearrange("p (c t) -> p c t", c=CP)
        shc = work[:, 1600:1984].rearrange("p (c t) -> p c t", c=CS)
        cand = work[:, 0:512].rearrange("p (h a b) -> p h a b", h=2, a=TOPK)
        left = work[:, 512:1024]
        onehot = [work[:, o:o + 512].rearrange("p (h s m) -> p h s m", h=2, s=TOPK) for o in (0, 512)]
        tv = work[:, 1408:1472].rearrange("p (h q k) -> p h q k", h=2, q=2)
        ti = work[:, 1472:1536].bitcast(U32).rearrange("p (h q k) -> p h q k", h=2, q=2)
        tif = work[:, 1536:1600].rearrange("p (h q k) -> p h q k", h=2, q=2)
        bj = work[:, 1600:1632].bitcast(U32).rearrange("p (h k) -> p h k", h=2)
        ab = work[:, 1632:1696].bitcast(U32).rearrange("p (q h k) -> p q h k", q=2, h=2)
        abf = work[:, 1696:1760].rearrange("p (q h k) -> p q h k", q=2, h=2)
        ij = work[:, 1760:1824].rearrange("p (q h k) -> p q h k", q=2, h=2)

        def h_of(item):
            return g_fin if item == TILES - 1 else h_cur

        psA, psB, psC, yacc = ps("psA"), ps("psB"), ps("psC"), ps("yacc")

        def tri(ap):
            return ap.rearrange("p (c t) -> p c t", t=P)

        p_gate, p_val = tri(psB[:, 0:384]), tri(psB[:, 512:896])
        p_u, p_sh = tri(psC[:, 0:256]), tri(psC[:, 512:896])
        p_sc, p_sb = tri(psA[:, 0:384]), tri(psA[:, 512:896])
        PROJ = []
        for dst, first, n in ((p_gate, DP + DC, CC), (p_val, DP, CC), (p_u, 0, CP),
                              (p_sh, DP + 2 * DC, CS), (p_sc, DP + 2 * DC + 2 * DSC, CS),
                              (p_sb, DP + 2 * DC + DSC, CS)):
            PROJ += [(first + c * P, dst, c) for c in range(n)]
        proj_of, last_chunk = {}, []
        for tick, n in PROJ_TICKS.items():
            done = last_chunk[-1] if last_chunk else 0
            proj_of[tick] = PROJ[done:done + n]
            last_chunk.append(done + n)
        assert last_chunk[-1] == len(PROJ) and last_chunk[:2] == [CC, 2 * CC]

        def proj_count(m, chunks):
            return len(last_chunk) * m + 1 + min(i for i, n in enumerate(last_chunk) if n >= chunks)

        TAPS = HC // CONV_TICKS + 1

        def taps_of(tick):
            return range(TAPS * (tick - CONV), min(TAPS * (tick - CONV + 1), HC + 1))

        GATE, VAL = CC, 2 * CC
        U = VAL + CP
        SH, SC, SB = U + CS, U + 2 * CS, U + 3 * CS
        STATE_CHUNKS = [(ubuf, c, HP) for c in range(CP)] + [(zbuf, c, HC) for c in range(CC)] + \
                       [(mbuf, c, HS) for c in range(CS)]

        s_const = sem("consts_made")
        s_fold = sem("fold_made")
        s_zero = sem("zeros_made")
        s_prm = sem("params_loaded")
        s_prmT = sem("params_turned")
        s_prmS = sem("params_stored")
        s_gfin = sem("g_final_loaded")
        s_wpz = sem("w_pool_cleared")
        s_wp = sem("w_pool_loaded")
        s_wi = [sem("w_in_loaded_gate"), sem("w_in_loaded_val"), sem("w_in_loaded_rest")]
        s_wo = sem("w_out_loaded")
        s_wq = sem("w_q_loaded")
        s_kst = sem("keys_loaded")
        s_ktT = sem("keys_turned")
        s_kT = sem("keys_stored")
        s_hst = sem("states_loaded")
        s_hstT = sem("states_turned")
        s_hist = sem("histories_set")
        s_x = sem("x_loaded")
        s_std1 = sem("x_std")
        s_inv1 = sem("x_std_inverted")
        s_xn = sem("x_normed")
        s_t1 = sem("x_turned")
        s_hT = sem("hT_set")
        s_proj = sem("projected")
        s_sig = sem("gate_sigmoid")
        s_zc = sem("conv_done")
        s_mean = sem("ln_sum")
        s_d = sem("ln_centred")
        s_sq = sem("ln_squared")
        s_var = sem("ln_sum_sq")
        s_lstd = sem("ln_std")
        s_xhat = sem("ln_normed")
        s_pd = sem("pool_diff")
        s_ya = sem("pool_mixed")
        s_sh = sem("s_h_copied")
        s_yp = sem("yT_pool_set")
        s_yb = sem("yT_conf_set")
        s_yc = sem("yT_short_set")
        s_yr = sem("yT_conf_repeated")
        s_nst = sem("new_states_turned")
        s_nsc = sem("new_states_copied")
        s_nso = sem("new_states_stored")
        s_wod = sem("w_out_done")
        s_x1 = sem("x_mixed")
        s_xst = sem("x_mixed_stored")
        s_std2 = sem("x1_std")
        s_inv2 = sem("x1_std_inverted")
        s_xn2 = sem("x1_normed")
        s_t2 = sem("x1_turned")
        s_hT2 = sem("ffn_hT_set")
        s_bt = sem("h_turned_back")
        s_h = sem("h_set")
        s_q = sem("queries_made")
        s_qT = sem("queries_copied")
        s_sc = sem("scores_made")
        s_e = sem("gate_logits")
        s_exp = sem("gate_exp")
        s_ids = sem("ids_ready")
        s_hcur = sem("h_cur_set")
        s_dots = sem("dots_copied")
        s_gelu = sem("gelu_done")
        s_coef = sem("coef_ready")
        s_urow = [sem(f"u_row_landed_{j}") for j in range(RING)]
        s_vrow = [sem(f"v_row_landed_{j}") for j in range(RING)]
        s_ufree = sem("u_rows_free")
        s_vfree = sem("v_rows_free")
        s_ustg = sem("u_indices_staged")
        s_vstg = sem("v_indices_staged")
        s_go = sem("pool_goes_on")
        s_coef4 = sem("coef4_staged")
        s_diag = sem("diag_made")
        s_ysum = sem("v_rows_summed")
        s_xo = sem("x_out_loaded")
        s_yend = sem("x_out_added")
        s_fstd = sem("final_std")
        s_fin = sem("final_normed")
        s_xost = sem("x_out_stored")
        dve_step = sem("dve_step")
        act_step = sem("act_step")

        block = ctx.enter_context(nc.Block())

        def rows_of(m):
            k = m % TILES
            return slice(k * P, k * P + width(m))

        def x_source(m):
            if m >= TILES:
                return x_mid[rows_of(m), :]
            if is_sample(m):
                return A["x_sample"][0, :, :]
            return A["x_prompt"][0, m * P:(m + 1) * P, :]

        def superstep(eng, n, spans, body, slices, mixer, extra):
            mixed = set(slices) if n + 1 < ITEMS else set()
            cuts = sorted({0, TICKS} | mixed | {e[0] for e in extra} | {t for s in spans for t in s[0:2]})
            for tick, upto in zip(cuts, cuts[1:] + [TICKS]):
                for _, work_of, args in (e for e in extra if e[0] == tick):
                    work_of(*args)
                if tick in mixed:
                    mixer(n + 1, tick)
                for span in spans:
                    item, (lo, hi) = span[2], part(span, tick, upto)
                    if hi - lo > 1:
                        with eng.Fori(0, hi - lo) as t:
                            body(item, t + lo)
                    elif hi > lo:
                        body(item, lo)

        @block.sync
        def _(sp):
            def load_w_in(l):
                for cols, s in ((slice(DP + DC, DP + 2 * DC), s_wi[0]), (slice(DP, DP + DC), s_wi[1]),
                                (slice(0, DP), s_wi[2]), (slice(DP + 2 * DC, D_IN), s_wi[2])):
                    sp.dma_start(w_in[:, :, cols], A["w_in"][l].rearrange("(c p) n -> p c n", p=P)[:, :, cols])\
                        .then_inc(s, 16)

            def load_w(dst, name, l, s):
                sp.dma_start(dst[:, :, :], A[name][l].rearrange("(c p) n -> p c n", p=P)).then_inc(s, 16)

            def load_keys(l):
                sp.dma_start(upper.rearrange("p (h q d) -> p h q d", h=HEADS, q=2),
                             A["sub_keys"][l].rearrange("h q n d -> n h q d")).then_inc(s_kst, 16)

            def load_x(m):
                if m >= TILES:
                    sp.wait_ge(s_xost, 16 * (m - TILES + 1))
                for q in range(loads(m)):
                    rows = width(m)
                    sp.dma_start(x_mix[q * rows:(q + 1) * rows, :], x_source(m)).then_inc(s_x, 16)

            def superstep_start(n):
                m = n + 1
                if m < ITEMS:
                    sp.wait_ge(s_hcur, n + 1)
                    load_x(m)
                    sp.wait_ge(s_ids, m)
                    if m % TILES == 0:
                        load_keys(m // TILES)
                    if is_sample(m):
                        l = m // TILES
                        sp.dma_start(upper[0:HP, 0:DP], A["state_pool"][l, 0]).then_inc(s_hst, 16)
                        sp.dma_start(upper[0:HC, DP:DP + DC], A["state_dwconv"][l, 0]).then_inc(s_hst, 16)
                        sp.dma_start(upper[0:HS, DP + DC:D], A["state_shortconv"][l, 0]).then_inc(s_hst, 16)

            def load_out(v):
                if v:
                    sp.wait_ge(s_xost, 16 * v)
                sp.wait_ge(s_xst, 16 * (v + 1))
                sp.dma_start(x_out[0:width(v), :], x_mid[rows_of(v), :]).then_inc(s_xo, 16)

            def store_out(v):
                if v < TILES:
                    sp.wait_ge(s_yend, v + 1)
                    dst = x_mid[rows_of(v), :]
                else:
                    sp.wait_ge(s_fin, v - TILES + 1)
                    k = v % TILES
                    dst = O["y_sample"][0] if is_sample(v) else O["y_prompt"][0, k * P:(k + 1) * P, :]
                sp.dma_start(dst, x_out[0:width(v), :]).then_inc(s_xost, 16)

            def mixer_io(m):
                l = m // TILES
                if outputs_state(m):
                    o = "sample" if is_sample(m) else "prompt"
                    sp.wait_ge(s_nsc, state_count(m))
                    sp.dma_start(O["new_pool_" + o][l, 0], upper[0:HP, 0:DP]).then_inc(s_nso, 16)
                    sp.dma_start(O["new_dwconv_" + o][l, 0], upper[0:HC, DP:DP + DC]).then_inc(s_nso, 16)
                    sp.dma_start(O["new_shortconv_" + o][l, 0], upper[0:HS, DP + DC:D]).then_inc(s_nso, 16)
                more = is_sample(m) and l + 1 < DEPTH
                if more:
                    sp.wait_ge(s_proj, proj_count(m, SB))
                    load_w_in(l + 1)
                sp.wait_ge(s_x1, m + 1)
                sp.dma_start(x_mid[rows_of(m), :], x_mix[0:width(m), :]).then_inc(s_xst, 16)
                if more:
                    sp.wait_ge(s_wod, m + 1)
                    load_w(w_out, "w_out", l + 1, s_wo)
                    sp.wait_ge(s_q, 2 * (m + 1))
                    load_w(w_q, "w_q", l + 1, s_wq)

            load_x(0)
            for l in range(DEPTH):
                taps = urows[0:NCH, 0, l * DC:(l + 1) * DC]
                sp.dma_start(taps[TAP:TAP + HC + 1, :], A["w_dw"][l]).then_inc(s_prm, 16)
                sp.dma_start(taps[BIAS:BIAS + 1, :], A["b_dw"][l:l + 1, :]).then_inc(s_prm, 16)
                sp.dma_start(taps[LNG:LNG + 1, :], A["ln_g"][l:l + 1, :]).then_inc(s_prm, 16)
                sp.dma_start(taps[LNB:LNB + 1, :], A["ln_b"][l:l + 1, :]).then_inc(s_prm, 16)
                sp.dma_start(taps[STAP:NCH, :], A["w_sc"][l]).then_inc(s_prm, 16)
                for name, r, n in (("g_mix", 0, DC8), ("g_ffn", DC8, DC8), ("pool_scale", 2 * DC8, CP)):
                    sp.dma_start(urows[r:r + n, 1, l * P:(l + 1) * P],
                                 A[name][l].rearrange("(c p) -> c p", p=P)).then_inc(s_prm, 16)
            load_keys(0)
            load_w_in(0)
            load_w(w_out, "w_out", 0, s_wo)
            sp.wait_ge(s_wpz, 1)
            for l in range(DEPTH):
                for g in range(len(WINDOWS)):
                    r = 64 * (g % 2)
                    sp.dma_start(w_pool[r:r + 64, l, g // 2, r:r + 64], A["w_pool"][l, g]).then_inc(s_wp, 16)
            load_w(w_q, "w_q", 0, s_wq)
            mixer_io(0)
            load_out(0)
            for n in range(ITEMS + 1):
                superstep_start(n)
                for early in (True, False):
                    for tick, v in v_ends(n):
                        if (tick < NORM2) == early:
                            store_out(v)
                            if v + 1 < ITEMS:
                                load_out(v + 1)
                    if early and n + 1 < ITEMS:
                        mixer_io(n + 1)
                if n == TILES:
                    sp.wait_ge(s_ufree, (before(n) + 1) * RING)
                    sp.dma_start(g_fin[:, :], A["g_final"].rearrange("(a d) -> a d", a=1).partition_broadcast(P))\
                        .then_inc(s_gfin, 16)
            sp.wait_ge(s_xost, 16 * ITEMS)
            sp.wait_ge(s_nso, 48 * state_count(ITEMS - 1))
            sp.wait_ge(s_xst, 16 * ITEMS)

        @block.gpsimd
        def _(pool):
            nc.gpsimd.memset(ident[:, :], 0.0).then_inc(s_go, 1)
            nc.gpsimd.iota(iota_i[:, :], pattern=[[1, TOPK]], base=0, channel_multiplier=0).then_inc(s_const, 1)
            nc.gpsimd.memset(w_pool[:, :, :, :], 0.0).then_inc(s_wpz, 1)
            pool.wait_ge(s_go, 1)
            nc.gpsimd.affine_select(out=ident[:, :], in_=ident[:, :], compare_op=ALU.not_equal, fill=1.0,
                                    base=0, pattern=[[-1, P]], channel_multiplier=1).then_inc(s_const, 1)

            def fetch_group(ring, item, group, parity):
                rows, table, idx, free, staged, landed = ring
                row = group * RING + before(item) * RING
                cols = slice(parity * RING, (parity + 1) * RING)
                for j in range(RING):
                    pool.wait_ge(free, row + (j + 1))
                    if j == 0:
                        nc.gpsimd.tensor_copy(idx[:, cols], ids[:, item % 3, bass.ds(group * RING, RING)])\
                            .then_inc(staged, 1)
                        pool.wait_ge(staged, group + (before(item) + 1))
                    pool.sem_inc(s_go, 1)
                    c = parity * RING + j
                    nc.gpsimd.indirect_dma_start(
                        out=rows[:, j, :], out_offset=None, in_=table[:, :],
                        in_offset=bass.IndirectOffsetOnAxis(ap=idx[:, c:c + 1], axis=0)).then_inc(landed[j], 16)
                    yield

            u_ring = (urows, eu, idx_u, s_ufree, s_ustg, s_urow)
            v_ring = (vrows, ev, idx_v, s_vfree, s_vstg, s_vrow)

            def groups_of(ring, item, group, count, odd=0):
                for g in range(count):
                    yield from fetch_group(ring, item, group + g, (odd + g) % 2)

            for n in range(ITEMS + 1):
                if n < ITEMS:
                    pool.wait_ge(s_ids, n + 1)
                streams = [(u_ring, s) for s in u_spans(n)] + [(v_ring, s) for s in v_spans(n)]
                cuts = sorted({t for _, s in streams for t in s[0:2]})
                for tick, upto in zip(cuts, cuts[1:]):
                    parts = []
                    for ring, span in streams:
                        lo, hi = part(span, tick, upto)
                        if hi > lo:
                            assert lo % 2 == 0 and hi % 2 == 0
                            parts.append((hi - lo, ring, span[2], lo))
                    if not parts:
                        continue
                    parts.sort(key=lambda p: p[0])
                    few = parts[0][0]
                    with pool.Fori(0, few // 2) as t:
                        for parity in range(2):
                            many = iter(())
                            if len(parts) == 2:
                                ratio = parts[1][0] // few
                                assert parts[1][0] == ratio * few
                                many = groups_of(*parts[1][1:3], t * (2 * ratio) + (parts[1][3] + parity * ratio),
                                                 ratio, parity * ratio)
                            for _ in groups_of(*parts[0][1:3], t * 2 + (parts[0][3] + parity), 1, parity):
                                for _ in range(ratio if len(parts) == 2 else 0):
                                    next(many)

        @block.scalar
        def _(act):
            steps = [0]

            def step(ins):
                ins.then_inc(act_step, 1)
                steps[0] += 1

            def settle():
                act.wait_ge(act_step, steps[0])

            def rms_std(src, out, rows, done):
                step(nc.scalar.activation(psA[0:rows, :], src, ACT.Square, accum_out=stat[0:rows, out:out + 1]))
                settle()
                nc.scalar.activation(stat[0:rows, out + 1:out + 2], stat[0:rows, out:out + 1], ACT.Sqrt,
                                     bias=eps[0:rows, :], scale=1.0 / D).then_inc(done, 1)

            def norm_rows(m, col, inverted, done):
                act.wait_ge(inverted, m + 1)
                nc.scalar.activation(xn, x_mix[:, :], ACT.Copy, scale=stat[:, col + 1:col + 2]).then_inc(done, 1)

            slices = (NORM, GATE_SIGMOID, SH_COPY, CENTRE, SCALE, NORM2, FFN_H, QUERY + 1, QUERY + 3, FINISH)

            def mixer(m, tick):
                l = m // TILES
                L = width(m)
                if tick == NORM:
                    act.wait_ge(s_x, 16 * sum(loads(i) for i in range(m + 1)))
                    if m == 0:
                        act.wait_ge(s_prmS, 2)
                    else:
                        act.wait_ge(s_qT, 2 * m)
                    rms_std(x_mix[:, :], 0, P, s_std1)
                    norm_rows(m, 0, s_inv1, s_xn)
                    if m % TILES == 0:
                        act.wait_ge(s_ktT, l + 1)
                        nc.scalar.copy(keysT[:, :, :], psC[:, :].rearrange("p (h n) -> p h n", h=HEADS))\
                            .then_inc(s_kT, 1)
                if tick == GATE_SIGMOID:
                    act.wait_ge(s_proj, proj_count(m, GATE))
                    act.wait_ge(s_t1, m + 1)
                    nc.scalar.activation(sig[:, :, 0:L], p_gate[:, :, 0:L], ACT.Sigmoid).then_inc(s_sig, 1)
                if tick == SH_COPY:
                    act.wait_ge(s_proj, proj_count(m, SH))
                    nc.scalar.copy(shc[:, :, 0:L], p_sh[:, :, 0:L]).then_inc(s_sh, 1)
                    act.wait_ge(s_ya, m + 1)
                    if m:
                        act.wait_ge(s_sc, 2 * m)
                    for c in range(CP):
                        step(nc.scalar.activation(yT[:, c, 0:L], psC[:, c * P:c * P + L], ACT.Copy,
                                                  scale=gain[:, l, 2 * DC8 + c:2 * DC8 + c + 1]))
                    settle()
                    act.sem_inc(s_yp, 1)
                if tick == CENTRE:
                    act.wait_ge(s_d, m + 1)
                    nc.scalar.activation(sig[:, :, 0:L], zc[:, :, 0:L], ACT.Square).then_inc(s_sq, 1)
                if tick == SCALE:
                    act.wait_ge(s_var, m + 1)
                    nc.scalar.activation(lnstd[:, 0:L], psB[:, 512:512 + L], ACT.Sqrt, bias=eps[:, :],
                                         scale=1.0 / DC).then_inc(s_lstd, 1)
                    act.wait_ge(s_xhat, m + 1)
                    for c in range(CC):
                        step(nc.scalar.activation(yT[:, CP + c, 0:L], zc[:, c, 0:L], ACT.Silu,
                                                  bias=chan[:, l, c, LNB:LNB + 1], scale=chan[:, l, c, LNG:LNG + 1]))
                    settle()
                    act.sem_inc(s_yb, 1)
                if tick == NORM2:
                    act.wait_ge(s_x1, m + 1)
                    rms_std(x_mix[:, :], 2, P, s_std2)
                    norm_rows(m, 2, s_inv2, s_xn2)
                if tick == FFN_H:
                    act.wait_ge(s_bt, m + 1)
                    act.wait_ge(s_xst, 16 * (m + 1))
                    step(nc.scalar.copy(x_mix[:, :], psC[:, :]))
                    settle()
                    act.sem_inc(s_h, 1)
                if tick in (QUERY + 1, QUERY + 3):
                    q = (tick - QUERY) // 2
                    act.wait_ge(s_q, 2 * m + q + 1)
                    nc.scalar.copy(qT[:, 4 * q:4 * q + 4, :],
                                   psA[:, 512 * q:512 * q + 512].rearrange("p (h t) -> p h t", t=P))\
                        .then_inc(s_qT, 1)
                if tick == FINISH:
                    act.wait_ge(s_e, m + 1)
                    nc.scalar.activation(best[:, :], best[:, :], ACT.Exp).then_inc(s_exp, 1)

            def superstep_start(n):
                if n < ITEMS:
                    if n >= 1 and h_of(n) is h_cur:
                        act.wait_ge(s_ufree, (before(n) + 1) * RING)
                    act.wait_ge(s_h, n + 1)
                    nc.scalar.copy(h_of(n)[:, :], x_mix[:, :]).then_inc(s_hcur, 1)

            def gelu_of(count, item, g0, g1):
                cols = slice(g0 * RING, g1 * RING)
                act.wait_ge(s_dots, before(item) + g1 + 1)
                if count:
                    act.wait_ge(s_coef, count)
                nc.scalar.activation(gelu[:, cols], dots[:, cols], ACT.Gelu).then_inc(s_gelu, 1)

            def final_std(v):
                act.wait_ge(s_yend, v + 1)
                if v + 1 < ITEMS:
                    act.wait_ge(s_qT, 2 * min(v + 3, ITEMS))
                rms_std(x_out[0:width(v), :], 4, width(v), s_fstd)

            def weights(item, group):
                row = group * RING + before(item) * RING
                act.wait_ge(s_diag, row + 1)
                nc.scalar.copy(coef4[:, :], coef[:, bass.ds(group * RING, RING)]).then_inc(s_coef4, 1)
                act.wait_ge(s_coef4, group + (before(item) + 1))
                for j in range(RING):
                    act.wait_ge(s_vfree, row + (j + 1))
                    nc.scalar.activation(diag[:, j, :], (fold if is_sample(item) else ident)[:, :], ACT.Copy,
                                         scale=coef4[:, j:j + 1]).then_inc(s_diag, 1)

            act.sem_inc(s_diag, 1)
            act.wait_ge(s_zero, 1)
            for tick in slices:
                mixer(0, tick)
            act.wait_ge(s_fold, 1)
            for n in range(ITEMS + 1):
                extra = []
                for tick, count, *what in weighings(n):
                    if tick == 0:
                        gelu_of(count, *what)
                        act.wait_ge(s_coef, count + 1)
                    else:
                        extra.append((tick, gelu_of, (count, *what)))
                        extra.append((tick + WEIGH_LAG, act.wait_ge, (s_coef, count + 1)))
                superstep_start(n)
                extra += [(FINAL_STD, final_std, (v,)) for _, v in v_ends(n) if v >= TILES]
                superstep(act, n, v_spans(n), weights, slices, mixer, extra)

        @block.tensor
        def _(pe):
            def turn(out, in_, rows=P):
                return nc.tensor.transpose(out, in_, ident[0:rows, 0:rows])

            def params():
                pe.wait_ge(s_const, 2)
                pe.wait_ge(s_prm, 16 * 8 * DEPTH)
                for l in range(DEPTH):
                    for c in range(CC):
                        o = (l * CC + c) * 64
                        turn(psB[:, o:o + NCH], urows[0:NCH, 0, l * DC + c * P:l * DC + (c + 1) * P], NCH)
                for l in range(DEPTH):
                    n = 2 * DC8 + CP
                    last = turn(psC[:, l * 64:l * 64 + n], urows[0:n, 1, l * P:(l + 1) * P], n)
                last.then_inc(s_prmT, 1)

            def queries(q):
                for h in range(2 * q, 2 * q + 2):
                    for c in range(DC8):
                        last = nc.tensor.matmul(psA[:, h * P:(h + 1) * P], w_q[:, c, h * P:(h + 1) * P],
                                                hT[:, c, :], start=c == 0, stop=c == DC8 - 1)
                if q % 2:
                    last.then_inc(s_q, 1)

            def scores(m, q):
                pe.wait_ge(s_qT, 2 * m + q + 1)
                dst = psC if q else psB
                for h in range(4):
                    for half in range(2):
                        r = slice(half * DH, (half + 1) * DH)
                        o = 512 * half + NK * h
                        last = nc.tensor.matmul(dst[:, o:o + NK], qT[r, 4 * q + h, :], keysT[r, 4 * q + h, :],
                                                start=True, stop=True)
                last.then_inc(s_sc, 1)

            def project_out(half, chunks, start, stop):
                o = 512 * half
                for c in chunks:
                    last = nc.tensor.matmul(psA[:, o:o + 512], yT[:, c, :], w_out[:, c, o:o + 512],
                                            start=start and c == chunks[0], stop=stop and c == chunks[-1])
                return last

            early = (*range(CP), *range(CP + CC, DC8))
            conf = tuple(range(CP, CP + CC))

            slices = (NORM, *PROJ_TICKS, CENTRE, SCALE, W_OUT, W_OUT + 1, NORM2,
                      *range(QUERY, QUERY + QUERY_TICKS))

            def mixer(m, tick):
                l = m // TILES
                L = width(m)
                if tick == NORM:
                    if m % TILES == 0:
                        pe.wait_ge(s_kst, 16 * (l + 1))
                        if m:
                            pe.wait_ge(s_ids, m)
                        else:
                            pe.wait_ge(s_prmS, 2)
                        for h in range(HEADS):
                            last = turn(psC[:, h * P:(h + 1) * P], upper[:, h * P:(h + 1) * P])
                        last.then_inc(s_ktT, 1)
                    if is_sample(m):
                        pe.wait_ge(s_hst, 48 * (l + 1))
                        pe.wait_ge(s_ids, m)
                        for i, (_, _, rows) in enumerate(STATE_CHUNKS):
                            last = turn(psC[:, i * 32:i * 32 + rows], upper[0:rows, i * P:(i + 1) * P], rows)
                        last.then_inc(s_hstT, 1)
                    pe.wait_ge(s_xn, m + 1)
                    for c in range(DC8):
                        last = turn(psA[:, c * P:(c + 1) * P], xn[:, c * P:(c + 1) * P])
                    last.then_inc(s_t1, 1)
                if tick in proj_of:
                    first = list(proj_of).index(tick)
                    if first == 0:
                        pe.wait_ge(s_hT, m + 1)
                        pe.wait_ge(s_wi[0], 16 * (l + 1))
                        if m:
                            pe.wait_ge(s_ids, m)
                    if last_chunk[first] > VAL and last_chunk[first - 1] <= VAL:
                        if is_sample(m):
                            pe.wait_ge(s_hist, l + 1)
                        pe.wait_ge(s_kT, l + 1)
                        pe.wait_ge(s_wi[2], 32 * (l + 1))
                    if last_chunk[first] == VAL:
                        pe.wait_ge(s_wi[1], 16 * (l + 1))
                    for col, dst, c in proj_of[tick]:
                        for k in range(DC8):
                            last = nc.tensor.matmul(dst[:, c, 0:L], w_in[:, k, col:col + P], hT[:, k, 0:L],
                                                    start=k == 0, stop=k == DC8 - 1)
                    last.then_inc(s_proj, 1)
                if tick == SH_COPY:
                    pe.wait_ge(s_wp, 16 * DEPTH * len(WINDOWS))
                    pe.wait_ge(s_pd, m + 1)
                    for c in range(CP):
                        last = nc.tensor.matmul(psC[:, c * P:c * P + L], w_pool[:, l, c, :], pdif[:, c, 0:L],
                                                start=True, stop=True)
                    last.then_inc(s_ya, 1)
                if tick == CENTRE:
                    pe.wait_ge(s_zc, m + 1)
                    for c in range(CC):
                        last = nc.tensor.matmul(psB[:, 0:L], ones[:, :], zc[:, c, 0:L],
                                                start=c == 0, stop=c == CC - 1)
                    last.then_inc(s_mean, 1)
                    pe.wait_ge(s_yp, m + 1)
                    pe.wait_ge(s_yc, m + 1)
                    pe.wait_ge(s_wo, 16 * (l + 1))
                    project_out(0, early, True, False)
                    pe.wait_ge(s_sq, m + 1)
                    for c in range(CC):
                        last = nc.tensor.matmul(psB[:, 512:512 + L], ones[:, :], sig[:, c, 0:L],
                                                start=c == 0, stop=c == CC - 1)
                    last.then_inc(s_var, 1)
                if tick == SCALE:
                    project_out(1, early, True, False)
                if tick == W_OUT:
                    if outputs_state(m):
                        for i, (buf, c, rows) in enumerate(STATE_CHUNKS):
                            last = turn(psC[0:rows, i * P:(i + 1) * P], buf[:, c, L:L + rows])
                        last.then_inc(s_nst, 1)
                    pe.wait_ge(s_yb, m + 1)
                    if is_sample(m):
                        pe.wait_ge(s_yr, l + 1)
                    project_out(0, conf, False, True)
                if tick == W_OUT + 1:
                    project_out(1, conf, False, True).then_inc(s_wod, 1)
                if tick == NORM2:
                    pe.wait_ge(s_xn2, m + 1)
                    for c in range(DC8):
                        last = turn(psB[:, c * P:(c + 1) * P], xn[:, c * P:(c + 1) * P])
                    last.then_inc(s_t2, 1)
                if tick == FFN_H:
                    pe.wait_ge(s_hT2, m + 1)
                    if outputs_state(m):
                        pe.wait_ge(s_nsc, state_count(m))
                    for c in range(DC8):
                        last = turn(psC[:, c * P:(c + 1) * P], hT[:, c, :])
                    last.then_inc(s_bt, 1)
                    pe.wait_ge(s_wq, 16 * (l + 1))
                if QUERY <= tick < QUERY + QUERY_TICKS:
                    pair = tick - QUERY
                    queries(pair)
                    if pair == 3:
                        pe.wait_ge(s_h, m + 1)
                    if pair % 2:
                        scores(m, pair // 2)

            def clear(start):
                for half in (0, 512):
                    last = nc.tensor.matmul(yacc[:, half:half + 512], zeros[:, 0:P], zeros[:, :],
                                            start=start, stop=not start, skip_group_check=True)
                return last

            def add_rows(item, group):
                row = group * RING + before(item) * RING
                for j in range(RING):
                    pe.wait_ge(s_vrow[j], group * 16 + (before(item) * 16 + 16))
                    pe.wait_ge(s_diag, row + (j + 2))
                    for half in (0, 512):
                        last = nc.tensor.matmul(yacc[:, half:half + 512], diag[:, j, :],
                                                vrows[:, j, half:half + 512], start=False, stop=False,
                                                skip_group_check=True)
                    last.then_inc(s_vfree, 1)

            pe.sem_inc(s_vfree, RING)
            params()
            for tick in slices:
                mixer(0, tick)
            pe.wait_ge(s_zero, 1)

            def open_sums(v):
                if v:
                    pe.wait_ge(s_yend, v)
                clear(True)

            def close_sums(v):
                clear(False).then_inc(s_ysum, 1)

            for n in range(ITEMS + 1):
                extra = [(tick, close_sums, (v,)) for tick, v in v_ends(n)] + \
                        [(tick, open_sums, (v,)) for tick, v in v_starts(n)]
                superstep(pe, n, v_spans(n), add_rows, slices, mixer, extra)

        @block.vector
        def _(dve):
            steps = [0]

            def step(ins):
                ins.then_inc(dve_step, 1)
                steps[0] += 1

            def settle(back=0):
                if steps[0] > back:
                    dve.wait_ge(dve_step, steps[0] - back)

            def chain(ins):
                step(ins)
                settle()

            def consts():
                nc.vector.memset(eps[:, :], EPS)
                nc.vector.memset(ones[:, :], 1.0)
                nc.vector.memset(zeros[:, :], 0.0)
                chain(nc.vector.memset(stat[:, :], 0.0))
                dve.sem_inc(s_zero, 1)
                dve.wait_ge(s_const, 2)
                for q in range(COPIES):
                    r = slice(q * LS, (q + 1) * LS)
                    step(nc.vector.tensor_copy(
                        fold[r, :].rearrange("p (q t) -> p q t", q=COPIES),
                        ident[r, r].unsqueeze(1).to_broadcast([LS, COPIES, LS])))
                chain(nc.vector.tensor_copy(iota_f[:, :], iota_i[:, :]))
                dve.sem_inc(s_fold, 1)
                for g, w in enumerate(WINDOWS):
                    r = slice(64 * (g % 2), 64 * (g % 2) + 64)
                    step(nc.vector.tensor_scalar(rcnt[r, g // 2, :], iota_f[r, :], 1.0, float(w), ALU.add, ALU.min))
                settle()
                chain(nc.vector.reciprocal(rcnt[:, :, :], rcnt[:, :, :]))
                dve.wait_ge(s_prmT, 1)
                nc.vector.tensor_copy(
                    chan[:, :, :, :].rearrange("p l c r -> p (l c) r"),
                    psB[:, 0:DEPTH * CC * 64].rearrange("p (g r) -> p g r", r=64)[:, :, 0:NCH]).then_inc(s_prmS, 1)
                nc.vector.tensor_copy(
                    gain[:, :, :],
                    psC[:, 0:DEPTH * 64].rearrange("p (g r) -> p g r", r=64)[:, :, 0:2 * DC8 + CP])\
                    .then_inc(s_prmS, 1)
                dve.wait_ge(s_prmS, 2)

            def invert_std(col, rows=P):
                return nc.vector.reciprocal(stat[0:rows, col + 1:col + 2], stat[0:rows, col + 1:col + 2])

            def scale_turned(ps_src, l, first):
                return nc.vector.tensor_tensor(
                    hT[:, :, :], ps_src[:, :].rearrange("p (c t) -> p c t", t=P),
                    gain[:, l, first:first + DC8].unsqueeze(2).to_broadcast([P, DC8, P]), ALU.mult)

            def taps(m, some):
                l, L = m // TILES, width(m)
                for k in some:
                    for c in range(CC):
                        z = zbuf[:, c, k:k + L]
                        w = chan[:, l, c, k:k + 1]
                        settle(CC - 1 if k else 0)
                        if k == 0:
                            step(nc.vector.tensor_scalar(zc[:, c, 0:L], z, w, chan[:, l, c, BIAS:BIAS + 1],
                                                         ALU.mult, ALU.add))
                        else:
                            step(nc.vector.scalar_tensor_tensor(out=zc[:, c, 0:L], in0=z, scalar=w,
                                                                in1=zc[:, c, 0:L], op0=ALU.mult, op1=ALU.add))

            def histories(m, which):
                for i, (buf, h) in enumerate(((ubuf, HP), (zbuf, HC), (mbuf, HS))):
                    if i not in which:
                        continue
                    if m % TILES == 0:
                        chain(nc.vector.memset(buf[:, :, 0:h], 0.0))
                    elif not is_sample(m):
                        chain(nc.vector.tensor_copy(buf[:, :, 0:h], buf[:, :, P:P + h]))

            def pool_windows(m):
                L = width(m)
                E = HP + L
                dve.wait_ge(s_proj, proj_count(m, U))
                chain(nc.vector.tensor_copy(ubuf[:, :, HP:E], p_u[:, :, 0:L]))
                chain(nc.vector.tensor_tensor(win_a[:, :, 1:E], ubuf[:, :, 1:E], ubuf[:, :, 0:E - 1], ALU.add))
                chain(nc.vector.tensor_tensor(win_b[:, :, 3:E], win_a[:, :, 3:E], win_a[:, :, 1:E - 2], ALU.add))
                chain(nc.vector.tensor_tensor(win_a[:, 1, 7:E], win_b[:, 1, 7:E], win_b[:, 1, 3:E - 4], ALU.add))
                chain(nc.vector.tensor_tensor(win_b[64:128, 1, 15:E], win_a[64:128, 1, 15:E],
                                              win_a[64:128, 1, 7:E - 8], ALU.add))
                sums = (win_a, win_b, win_a, win_b)
                for g, w in enumerate(WINDOWS):
                    r, c = slice(64 * (g % 2), 64 * (g % 2) + 64), g // 2
                    step(nc.vector.scalar_tensor_tensor(
                        out=pdif[r, c, 0:L], in0=sums[g][r, c, HP:E], scalar=1.0 / w,
                        in1=ubuf[r, c, HP:E], op0=ALU.mult, op1=ALU.subtract))
                settle()
                if m % TILES == 0:
                    for g in range(len(WINDOWS)):
                        r, c = slice(64 * (g % 2), 64 * (g % 2) + 64), g // 2
                        step(nc.vector.tensor_tensor(pdif[r, c, 0:TOPK], sums[g][r, c, HP:HP + TOPK],
                                                     rcnt[r, c, :], ALU.mult))
                    settle()
                    chain(nc.vector.tensor_tensor(pdif[:, :, 0:TOPK], pdif[:, :, 0:TOPK],
                                                  ubuf[:, :, HP:HP + TOPK], ALU.subtract))
                dve.sem_inc(s_pd, 1)

            def repeat(first, end):
                step(nc.vector.tensor_copy(
                    yT[:, first:end, LS:P].rearrange("p c (q t) -> p c q t", t=LS),
                    yT[:, first:end, 0:LS].unsqueeze(2).to_broadcast([P, end - first, COPIES - 1, LS])))

            def short_conv(m):
                l, L = m // TILES, width(m)
                dve.wait_ge(s_sh, m + 1)
                dve.wait_ge(s_proj, proj_count(m, SB))
                if m:
                    dve.wait_ge(s_sc, 2 * m)
                chain(nc.vector.tensor_tensor(mbuf[:, :, HS:HS + L], p_sc[:, :, 0:L], shc[:, :, 0:L], ALU.mult))
                for k in range(HS + 1):
                    for c in range(CS):
                        x, w = mbuf[:, c, k:k + L], chan[:, l, c, STAP + k:STAP + k + 1]
                        settle(CS - 1 if k else 0)
                        if k == 0:
                            step(nc.vector.tensor_scalar(shc[:, c, 0:L], x, w, None, ALU.mult))
                        else:
                            step(nc.vector.scalar_tensor_tensor(out=shc[:, c, 0:L], in0=x, scalar=w,
                                                                in1=shc[:, c, 0:L], op0=ALU.mult, op1=ALU.add))
                settle()
                step(nc.vector.tensor_tensor(yT[:, CP + CC:DC8, 0:L], p_sb[:, :, 0:L], shc[:, :, 0:L], ALU.mult))
                settle()
                if is_sample(m):
                    dve.wait_ge(s_yp, m + 1)
                    repeat(0, CP)
                    repeat(CP + CC, DC8)
                    settle()
                dve.sem_inc(s_yc, 1)

            def top16(rows):
                back = len(rows) - 1
                n = 512 // len(rows)
                rest = [left[:, i * n:i * n + values.shape[-1]] for i, (values, _, _) in enumerate(rows)]
                for values, out_v, _ in rows:
                    step(nc.vector.max(out_v[:, 0:8], values))
                for values, out_v, out_i in rows:
                    settle(back)
                    step(nc.vector.max_index(out_i[:, 0:8], out_v[:, 0:8], values))
                for (values, out_v, _), r in zip(rows, rest):
                    step(nc.vector.match_replace(r, out_v[:, 0:8], values, LOWEST))
                for (_, out_v, _), r in zip(rows, rest):
                    settle(back)
                    step(nc.vector.max(out_v[:, 8:16], r))
                for (_, out_v, out_i), r in zip(rows, rest):
                    settle(back)
                    step(nc.vector.max_index(out_i[:, 8:16], out_v[:, 8:16], r))
                settle()

            def top_keys(m, pair):
                q = pair // 2
                src = psC if q else psB
                dve.wait_ge(s_sc, 2 * m + q + 1)
                if pair == 0 and outputs_state(m):
                    dve.wait_ge(s_nso, 48 * state_count(m))
                top16([(src[:, o:o + NK], tv[:, h, half, :], ti[:, h, half, :])
                       for h in range(2) for half in range(2)
                       for o in (512 * half + NK * (2 * (pair % 2) + h),)])
                chain(nc.vector.tensor_copy(tif[:, :, :, :], ti[:, :, :, :]))

            def top_sums(m, pair):
                for h in range(2):
                    step(nc.vector.tensor_tensor(
                        cand[:, h, :, :], tv[:, h, 0, :].unsqueeze(2).to_broadcast([P, TOPK, TOPK]),
                        tv[:, h, 1, :].unsqueeze(1).to_broadcast([P, TOPK, TOPK]), ALU.add))
                settle()
                top16([(cand[:, h, :, :].rearrange("p a b -> p (a b)"),
                        best[:, (2 * pair + h) * TOPK:(2 * pair + h + 1) * TOPK], bj[:, h, :])
                       for h in range(2)])

            def experts(m, pair):
                step(nc.vector.tensor_scalar(ab[:, 0, :, :], bj[:, :, :], 4, None, ALU.logical_shift_right))
                step(nc.vector.tensor_scalar(ab[:, 1, :, :], bj[:, :, :], TOPK - 1, None, ALU.bitwise_and))
                settle()
                chain(nc.vector.tensor_copy(abf[:, :, :, :], ab[:, :, :, :]))
                for half in range(2):
                    step(nc.vector.tensor_tensor(
                        onehot[half], abf[:, half, :, :].unsqueeze(3).to_broadcast([P, 2, TOPK, TOPK]),
                        iota_f[:, :].unsqueeze(1).unsqueeze(1).to_broadcast([P, 2, TOPK, TOPK]), ALU.is_equal))
                for half in range(2):
                    settle(1)
                    step(nc.vector.tensor_tensor(
                        onehot[half], onehot[half],
                        tif[:, :, half, :].unsqueeze(2).to_broadcast([P, 2, TOPK, TOPK]), ALU.mult))
                for half in range(2):
                    settle(1)
                    step(nc.vector.tensor_reduce(ij[:, half, :, :], onehot[half], AX.X, ALU.add))
                settle()
                o = 2 * pair * TOPK
                chain(nc.vector.scalar_tensor_tensor(
                    out=idf[:, o:o + 2 * TOPK], in0=ij[:, 0, :, :].rearrange("p h k -> p (h k)"),
                    scalar=float(NK), in1=ij[:, 1, :, :].rearrange("p h k -> p (h k)"),
                    op0=ALU.mult, op1=ALU.add))

            def finish_routing(m):
                b3 = best[:, :].rearrange("p (h k) -> p h k", k=TOPK)
                chain(nc.vector.tensor_copy(hsum[:, :], b3[:, :, 0]))
                chain(nc.vector.tensor_tensor(b3, b3, hsum[:, :].unsqueeze(2).to_broadcast([P, HEADS, TOPK]),
                                              ALU.subtract))
                dve.sem_inc(s_e, 1)
                base = float(m // TILES * NE)
                spans = [(slice(q * LS, (q + 1) * LS), slice(q * 32, q * 32 + 32)) for q in range(COPIES)] \
                    if is_sample(m) else [(slice(0, P), slice(0, KPICK))]
                for r, cols in spans:
                    n = cols.stop - cols.start
                    step(nc.vector.tensor_scalar(ids[r, m % 3, 0:n], idf[r, cols], base, None, ALU.add))
                dve.wait_ge(s_exp, m + 1)
                chain(nc.vector.tensor_reduce(hsum[:, :], b3, AX.X, ALU.add))
                chain(nc.vector.reciprocal(hsum[:, :], hsum[:, :]))
                chain(nc.vector.tensor_tensor(b3, b3, hsum[:, :].unsqueeze(2).to_broadcast([P, HEADS, TOPK]),
                                              ALU.mult))
                for r, cols in spans:
                    n = cols.stop - cols.start
                    step(nc.vector.tensor_copy(gates[r, m % 2, 0:n], best[r, cols]))
                settle()
                dve.sem_inc(s_ids, 1)

            slices = (NORM, *range(CONV, CONV + CONV_TICKS), CENTRE, SCALE, W_OUT, W_OUT + 2, NORM2, FFN_H,
                      *range(ROUTE, ROUTE + 3 * HEADS // 2), FINISH)

            def mixer(m, tick):
                l, L = m // TILES, width(m)
                if tick == NORM:
                    dve.wait_ge(s_std1, m + 1)
                    invert_std(0).then_inc(s_inv1, 1)
                    if is_sample(m):
                        dve.wait_ge(s_hstT, l + 1)
                        ph = psC[:, 0:256].rearrange("p (i t) -> p i t", t=32)
                        step(nc.vector.tensor_copy(ubuf[:, :, 0:HP], ph[:, 0:CP, 0:HP]))
                        step(nc.vector.tensor_copy(zbuf[:, :, 0:HC], ph[:, CP:CP + CC, 0:HC]))
                        step(nc.vector.tensor_copy(mbuf[:, :, 0:HS], ph[:, CP + CC:DC8, 0:HS]))
                        settle()
                        dve.sem_inc(s_hist, 1)
                    dve.wait_ge(s_t1, m + 1)
                    scale_turned(psA, l, 0).then_inc(s_hT, 1)
                if tick == CONV:
                    histories(m, (1,))
                    dve.wait_ge(s_sig, m + 1)
                    dve.wait_ge(s_proj, proj_count(m, VAL))
                    chain(nc.vector.tensor_tensor(zbuf[:, :, HC:HC + L], p_val[:, :, 0:L], sig[:, :, 0:L], ALU.mult))
                if tick == POOLING:
                    histories(m, (0, 2))
                    pool_windows(m)
                if CONV <= tick < CONV + CONV_TICKS:
                    taps(m, taps_of(tick))
                    if tick == CONV + CONV_TICKS - 1:
                        settle()
                        dve.sem_inc(s_zc, 1)
                if tick == SHORT:
                    short_conv(m)
                if tick == CENTRE:
                    dve.wait_ge(s_mean, m + 1)
                    nc.vector.scalar_tensor_tensor(
                        out=zc[:, :, 0:L], in0=psB[:, 0:L].unsqueeze(1).to_broadcast([P, CC, L]),
                        scalar=-1.0 / DC, in1=zc[:, :, 0:L], op0=ALU.mult, op1=ALU.add).then_inc(s_d, 1)
                if tick == SCALE:
                    dve.wait_ge(s_lstd, m + 1)
                    chain(nc.vector.reciprocal(lnstd[:, 0:L], lnstd[:, 0:L]))
                    nc.vector.tensor_tensor(zc[:, :, 0:L], zc[:, :, 0:L],
                                            lnstd[:, 0:L].unsqueeze(1).to_broadcast([P, CC, L]), ALU.mult)\
                        .then_inc(s_xhat, 1)
                if tick == W_OUT and is_sample(m):
                    dve.wait_ge(s_yb, m + 1)
                    repeat(CP, CP + CC)
                    settle()
                    dve.sem_inc(s_yr, 1)
                if tick == W_OUT + 2 and outputs_state(m):
                    dve.wait_ge(s_nst, state_count(m))
                    for rows, cols in ((HP, slice(0, DP)), (HC, slice(DP, DP + DC)), (HS, slice(DP + DC, D))):
                        step(nc.vector.tensor_copy(upper[0:rows, cols], psC[0:rows, cols]))
                    settle()
                    dve.sem_inc(s_nsc, 1)
                if tick == NORM2:
                    dve.wait_ge(s_wod, m + 1)
                    nc.vector.tensor_tensor(x_mix[:, :], psA[:, :], x_mix[:, :], ALU.add).then_inc(s_x1, 1)
                    dve.wait_ge(s_std2, m + 1)
                    invert_std(2).then_inc(s_inv2, 1)
                if tick == FFN_H:
                    dve.wait_ge(s_t2, m + 1)
                    scale_turned(psB, l, DC8).then_inc(s_hT2, 1)
                if ROUTE <= tick < FINISH:
                    pair, stage = divmod(tick - ROUTE, 3)
                    (top_keys, top_sums, experts)[stage](m, pair)
                if tick == FINISH:
                    finish_routing(m)

            def take_sums(v):
                rows = width(v)
                dve.wait_ge(s_ysum, v + 1)
                dve.wait_ge(s_xo, 16 * (v + 1))
                nc.vector.tensor_tensor(x_out[0:rows, :], yacc[0:rows, :], x_out[0:rows, :], ALU.add)\
                    .then_inc(s_yend, 1)

            def final_norm(v):
                rows = width(v)
                dve.wait_ge(s_gfin, 16)
                dve.wait_ge(s_fstd, v - TILES + 1)
                chain(invert_std(4, rows))
                nc.vector.scalar_tensor_tensor(out=x_out[0:rows, :], in0=x_out[0:rows, :],
                                               scalar=stat[0:rows, 5:6], in1=g_fin[0:rows, :],
                                               op0=ALU.mult, op1=ALU.mult).then_inc(s_fin, 1)

            def weigh(count, item, g0, g1):
                cols = slice(g0 * RING, g1 * RING)
                dve.wait_ge(s_gelu, count + 1)
                if item:
                    dve.wait_ge(s_coef4, before(item - 1) + min(g1, groups(item - 1)))
                nc.vector.tensor_tensor(coef[:, cols], gelu[:, cols], gates[:, item % 2, cols], ALU.mult)\
                    .then_inc(s_coef, 1)

            def dot_rows(item, group):
                row = group * RING + before(item) * RING
                dve.wait_ge(s_dots, group + (before(item) + 1))
                for j in range(RING):
                    dve.wait_ge(s_urow[j], group * 16 + (before(item) * 16 + 16))
                    nc.vector.tensor_tensor_reduce(urows[:, j, :], urows[:, j, :], h_of(item)[:, :], 1.0, 0.0,
                                                   ALU.mult, ALU.add, dots4[:, j:j + 1]).then_inc(s_ufree, 1)
                dve.wait_ge(s_ufree, row + 2 * RING)
                nc.vector.tensor_copy(dots[:, bass.ds(group * RING, RING)], dots4[:, :]).then_inc(s_dots, 1)

            dve.sem_inc(s_ufree, RING)
            dve.sem_inc(s_dots, 1)
            consts()
            for tick in slices:
                mixer(0, tick)
            for n in range(ITEMS + 1):
                extra = []
                for tick, count, *what in weighings(n):
                    if tick == 0:
                        weigh(count, *what)
                    else:
                        extra.append((tick + 1, weigh, (count, *what)))
                if n < ITEMS:
                    dve.wait_ge(s_hcur, n + 1)
                extra += [(tick, take_sums, (v,)) for tick, v in v_ends(n)]
                extra += [(FINAL_NORM, final_norm, (v,)) for _, v in v_ends(n) if v >= TILES]
                superstep(dve, n, u_spans(n), dot_rows, slices, mixer, extra)


_INS = ['x_prompt', 'x_sample', 'state_pool', 'state_dwconv', 'state_shortconv', 'g_mix', 'w_in', 'w_pool',
        'pool_scale', 'w_dw', 'b_dw', 'ln_g', 'ln_b', 'w_sc', 'w_out', 'g_ffn', 'w_q', 'sub_keys', 'expert_u',
        'expert_v', 'g_final']
_OUTS = ['y_prompt', 'y_sample', 'new_pool_prompt', 'new_dwconv_prompt', 'new_shortconv_prompt',
         'new_pool_sample', 'new_dwconv_sample', 'new_shortconv_sample']


def kernel(**inputs):
    import numpy as _np
    import concourse.bacc as _bacc
    from concourse import mybir as _mybir
    from concourse.bass_utils import run_bass_kernel_spmd as _run

    nc = _bacc.Bacc("TRN2", target_bir_lowering=False, num_devices=1, dynamic_dma_scratch_size=4096)
    arrays, ins, outs = {}, {}, {}
    for name in _INS:
        a = _np.ascontiguousarray(inputs[name])
        arrays[f"in_{name}"] = a
        ins[name] = nc.dram_tensor(f"in_{name}", a.shape, _mybir.dt.from_np(a.dtype), kind="ExternalInput").ap()
    shape = {n: inputs[n].shape for n in _INS}
    batch = shape['x_prompt'][0]
    out_shapes = [shape['x_prompt'], shape['x_sample']]
    for _ in range(2):
        out_shapes += [(s[0], batch) + tuple(s[2:]) for s in
                       (shape['state_pool'], shape['state_dwconv'], shape['state_shortconv'])]
    for name, s in zip(_OUTS, out_shapes):
        outs[name] = nc.dram_tensor(f"out_{name}", tuple(s), _mybir.dt.float32, kind="ExternalOutput").ap()
    build(nc, ins, outs)
    r = _run(nc, [arrays], core_ids=[0])
    return tuple(r.results[0][f"out_{name}"] for name in _OUTS)
```
